# Optimizing a Trainium2 kernel written in Bass

```python
import jax, jax.numpy as jnp
from jax import lax
import numpy as np

D_MODEL = 2048
BATCH = 1
SEQ = 256
DEPTH = 1
DEC_BATCH = 8
DEC_SEQ = 4
PAST_LEN = 2048
PAGE_SIZE = 128

HG_HEADS = 16
HG_KDIM = 128
HG_VDIM = D_MODEL // HG_HEADS
HG_CHUNK = 64
ML_HEADS = 8
ML_VDIM = D_MODEL // ML_HEADS
ML_QKDIM = ML_VDIM // 2
ML_CHUNK = 64
D_FF = ((8 * D_MODEL // 3 + 255) // 256) * 256
CONV_W = 3
EPS = 1e-6

HG_KW = HG_HEADS * HG_KDIM
HG_VW = HG_HEADS * HG_VDIM
ML_QKW = ML_HEADS * ML_QKDIM
ML_VW = ML_HEADS * ML_VDIM
IN_SPLITS = (HG_KW, HG_KW, HG_VW, HG_VW, ML_QKW, ML_QKW, ML_VW, ML_HEADS, ML_HEADS, ML_VW, D_MODEL, D_MODEL)
D_IN = sum(IN_SPLITS)

kernel_name = 'hgrn2_mlstm_convffn_adaln_step'

def rms_norm(x, w=None):
    x32 = x.astype(jnp.float32)
    y = x32 * lax.rsqrt(jnp.mean(x32 * x32, axis=-1, keepdims=True) + EPS)
    if w is not None:
        y = y * w.astype(jnp.float32)
    return y.astype(x.dtype)

def head_rms_norm(x, w):
    B, T, H, Dh = x.shape
    y = x * lax.rsqrt(jnp.mean(x * x, axis=-1, keepdims=True) + EPS)
    return y.reshape(B, T, H * Dh) * w.astype(jnp.float32)

def to_chunks(a, L, fill):
    B, T = a.shape[:2]
    pad = (-T) % L
    a = jnp.pad(a, [(0, 0), (0, pad)] + [(0, 0)] * (a.ndim - 2), constant_values=fill)
    n = a.shape[1] // L
    a = a.reshape((B, n, L) + a.shape[2:])
    perm = (1, 0, 3, 2) + tuple(range(4, a.ndim))
    return a.transpose(perm)

def from_chunks(o, T):
    n, B, H, L, V = o.shape
    return o.transpose(1, 0, 3, 2, 4).reshape(B, n * L, H, V)[:, :T]

def hgrn2_chunked(q, k, logf, v, S0):
    T = q.shape[1]
    L = min(HG_CHUNK, T)
    causal = jnp.tril(jnp.ones((L, L), dtype=bool))

    def step(S, blk):
        qc, kc, gc, vc = blk
        b = jnp.cumsum(gc, axis=2)
        diff = jnp.where(causal[None, None, :, :, None], b[:, :, :, None, :] - b[:, :, None, :, :], -jnp.inf)
        A = jnp.einsum('bhtk,bhtsk,bhsk->bhts', qc, jnp.exp(diff), kc)
        o = jnp.einsum('bhtk,bhkv->bhtv', qc * jnp.exp(b), S) + jnp.einsum('bhts,bhsv->bhtv', A, vc)
        bL = b[:, :, -1:, :]
        S = jnp.exp(bL[:, :, 0, :])[..., None] * S + jnp.einsum('bhsk,bhsv->bhkv', kc * jnp.exp(bL - b), vc)
        return S, o

    S, o = lax.scan(step, S0, (to_chunks(q, L, 0.0), to_chunks(k, L, 0.0), to_chunks(logf, L, 0.0), to_chunks(v, L, 0.0)))
    return from_chunks(o, T), S

def mlstm_chunked(q, k, v, ig, lf, C0, n0, m0):
    T = q.shape[1]
    L = min(ML_CHUNK, T)
    causal = jnp.tril(jnp.ones((L, L), dtype=bool))

    def step(carry, blk):
        C, n, m = carry
        qc, kc, vc, igc, lfc = blk
        b = jnp.cumsum(lfc, axis=-1)
        Dm = jnp.where(causal, b[..., :, None] - b[..., None, :] + igc[..., None, :], -jnp.inf)
        mt = jnp.maximum(b + m[..., None], jnp.max(Dm, axis=-1))
        inter = jnp.exp(b + m[..., None] - mt)
        Sc = jnp.einsum('bhtd,bhsd->bhts', qc, kc) * jnp.exp(Dm - mt[..., None])
        num = inter[..., None] * jnp.einsum('bhtd,bhdv->bhtv', qc, C) + jnp.einsum('bhts,bhsv->bhtv', Sc, vc)
        den = inter * jnp.einsum('bhtd,bhd->bht', qc, n) + jnp.sum(Sc, axis=-1)
        h = num / jnp.maximum(jnp.abs(den), jnp.exp(-mt))[..., None]
        mL = mt[..., -1]
        decL = jnp.exp(b[..., -1] + m - mL)
        wk = jnp.exp(b[..., -1:] - b + igc - mL[..., None])
        C = decL[..., None, None] * C + jnp.einsum('bhs,bhsd,bhsv->bhdv', wk, kc, vc)
        n = decL[..., None] * n + jnp.einsum('bhs,bhsd->bhd', wk, kc)
        return (C, n, mL), h

    (C, n, m), h = lax.scan(step, (C0, n0, m0), (to_chunks(q, L, 0.0), to_chunks(k, L, 0.0), to_chunks(v, L, 0.0),
                                                 to_chunks(ig, L, -jnp.inf), to_chunks(lf, L, 0.0)))
    return from_chunks(h, T), C, n, m

def token_mixer(h, st_hg, st_C, st_n, st_m, w_in, lb, hg_norm_w, ml_i_bias, ml_f_bias, ml_norm_w, w_out):
    f32 = jnp.float32
    B, T, _ = h.shape
    proj = h @ w_in
    hq, hf, hi, hg, mq, mk, mv, mi, mf, mo, ga, gb = jnp.split(proj, list(np.cumsum(IN_SPLITS)[:-1]), axis=-1)
    lb = lb.reshape(HG_HEADS, HG_KDIM)
    z = hf.astype(f32).reshape(B, T, HG_HEADS, HG_KDIM)
    logf = jnp.log(lb + (1.0 - lb) * jax.nn.sigmoid(z))
    kk = (1.0 - lb) * jax.nn.sigmoid(-z)
    q = jax.nn.silu(hq.astype(f32)).reshape(B, T, HG_HEADS, HG_KDIM) * (HG_KDIM ** -0.5)
    vv = hi.astype(f32).reshape(B, T, HG_HEADS, HG_VDIM)
    o_hg, S_new = hgrn2_chunked(q, kk, logf, vv, st_hg.astype(f32))
    y_a = head_rms_norm(o_hg, hg_norm_w) * jax.nn.silu(hg.astype(f32))
    mq_ = mq.astype(f32).reshape(B, T, ML_HEADS, ML_QKDIM) * (ML_QKDIM ** -0.5)
    mk_ = mk.astype(f32).reshape(B, T, ML_HEADS, ML_QKDIM)
    mv_ = mv.astype(f32).reshape(B, T, ML_HEADS, ML_VDIM)
    ig = mi.astype(f32) + ml_i_bias.astype(f32)
    lf = jax.nn.log_sigmoid(mf.astype(f32) + ml_f_bias.astype(f32))
    h_ml, C_new, n_new, m_new = mlstm_chunked(mq_, mk_, mv_, ig, lf, st_C.astype(f32), st_n.astype(f32), st_m.astype(f32))
    y_b = head_rms_norm(h_ml, ml_norm_w) * jax.nn.sigmoid(mo.astype(f32))
    merged = jax.nn.sigmoid(ga.astype(f32)) * y_a + jax.nn.sigmoid(gb.astype(f32)) * y_b
    out = merged.astype(h.dtype) @ w_out
    return (out, S_new.astype(st_hg.dtype), C_new.astype(st_C.dtype), n_new.astype(st_n.dtype), m_new.astype(st_m.dtype))

def conv_ffn(h, conv_state, conv_w, conv_b, w_up, w_down):
    T = h.shape[1]
    up = h @ w_up
    a, g = up[..., :D_FF], up[..., D_FF:]
    full = jnp.concatenate([conv_state.astype(a.dtype), a], axis=1)
    a_conv = sum(conv_w[j] * full[:, j:j + T] for j in range(CONV_W)) + conv_b
    y = jax.nn.gelu(a_conv, approximate=False) * g
    return y @ w_down, full[:, -(CONV_W - 1):]

def trunk(x, c, st_hg, st_C, st_n, st_m, st_conv, ada_w, ada_b, w_in, hg_lb_logits, hg_norm_w, ml_i_bias,
          ml_f_bias, ml_norm_w, w_out, conv_w, conv_b, w_up, w_down, final_norm_w):
    lbs = jnp.cumsum(jax.nn.softmax(hg_lb_logits.astype(jnp.float32), axis=0), axis=0)
    hg_l, C_l, n_l, m_l, cv_l = [], [], [], [], []
    for l in range(DEPTH):
        mod = jax.nn.silu(c) @ ada_w[l] + ada_b[l]
        sh1, sc1, g1, sh2, sc2, g2 = jnp.split(mod[:, None, :], 6, axis=-1)
        h = rms_norm(x) * (1.0 + sc1) + sh1
        mix, s_hg, s_C, s_n, s_m = token_mixer(h, st_hg[l], st_C[l], st_n[l], st_m[l], w_in[l], lbs[l],
                                               hg_norm_w[l], ml_i_bias[l], ml_f_bias[l], ml_norm_w[l], w_out[l])
        x = x + g1 * mix
        h = rms_norm(x) * (1.0 + sc2) + sh2
        ff, s_cv = conv_ffn(h, st_conv[l], conv_w[l], conv_b[l], w_up[l], w_down[l])
        x = x + g2 * ff
        hg_l.append(s_hg); C_l.append(s_C); n_l.append(s_n); m_l.append(s_m); cv_l.append(s_cv)
    y = rms_norm(x, final_norm_w)
    return y, jnp.stack(hg_l), jnp.stack(C_l), jnp.stack(n_l), jnp.stack(m_l), jnp.stack(cv_l)

def setup_inputs(seed: int = 0) -> dict:
    key = jax.random.key(seed)
    ks = jax.random.split(key, 24)
    nrm = lambda k, shape, s: jax.random.normal(k, shape, jnp.float32) * s
    D = D_MODEL
    return {
        'x_prompt': nrm(ks[0], (BATCH, SEQ, D), 1.0),
        'x_sample': nrm(ks[1], (DEC_BATCH, DEC_SEQ, D), 1.0),
        'c_prompt': nrm(ks[2], (BATCH, D), 1.0),
        'c_sample': nrm(ks[3], (DEC_BATCH, D), 1.0),
        'state_hgrn': nrm(ks[4], (DEPTH, DEC_BATCH, HG_HEADS, HG_KDIM, HG_VDIM), 0.5),
        'state_mlstm_C': nrm(ks[5], (DEPTH, DEC_BATCH, ML_HEADS, ML_QKDIM, ML_VDIM), 0.5),
        'state_mlstm_n': nrm(ks[6], (DEPTH, DEC_BATCH, ML_HEADS, ML_QKDIM), 0.5),
        'state_mlstm_m': nrm(ks[7], (DEPTH, DEC_BATCH, ML_HEADS), 1.0),
        'state_conv': nrm(ks[8], (DEPTH, DEC_BATCH, CONV_W - 1, D_FF), 1.0),
        'ada_w': nrm(ks[9], (DEPTH, D, 6 * D), 0.5 * D ** -0.5),
        'ada_b': nrm(ks[10], (DEPTH, 6 * D), 0.02),
        'w_in': nrm(ks[11], (DEPTH, D, D_IN), D ** -0.5),
        'hg_lb_logits': nrm(ks[12], (DEPTH + 1, HG_KW), 0.1),
        'hg_norm_w': 1.0 + nrm(ks[13], (DEPTH, HG_VW), 0.02),
        'ml_i_bias': nrm(ks[14], (DEPTH, ML_HEADS), 0.1),
        'ml_f_bias': jnp.linspace(3.0, 6.0, ML_HEADS, dtype=jnp.float32)[None, :] + nrm(ks[15], (DEPTH, ML_HEADS), 0.1),
        'ml_norm_w': 1.0 + nrm(ks[16], (DEPTH, ML_VW), 0.02),
        'w_out': nrm(ks[17], (DEPTH, D, D), D ** -0.5),
        'conv_w': nrm(ks[18], (DEPTH, CONV_W, D_FF), CONV_W ** -0.5),
        'conv_b': nrm(ks[19], (DEPTH, D_FF), 0.02),
        'w_up': nrm(ks[20], (DEPTH, D, 2 * D_FF), D ** -0.5),
        'w_down': nrm(ks[21], (DEPTH, D_FF, D), D_FF ** -0.5),
        'final_norm_w': 1.0 + nrm(ks[22], (D,), 0.02),
    }

def reference(x_prompt, x_sample, c_prompt, c_sample, state_hgrn, state_mlstm_C, state_mlstm_n, state_mlstm_m,
              state_conv, ada_w, ada_b, w_in, hg_lb_logits, hg_norm_w, ml_i_bias, ml_f_bias, ml_norm_w, w_out,
              conv_w, conv_b, w_up, w_down, final_norm_w):
    dt = x_prompt.dtype
    z_hg = jnp.zeros((DEPTH, BATCH, HG_HEADS, HG_KDIM, HG_VDIM), dt)
    z_C = jnp.zeros((DEPTH, BATCH, ML_HEADS, ML_QKDIM, ML_VDIM), dt)
    z_n = jnp.zeros((DEPTH, BATCH, ML_HEADS, ML_QKDIM), dt)
    z_m = jnp.zeros((DEPTH, BATCH, ML_HEADS), dt)
    z_cv = jnp.zeros((DEPTH, BATCH, CONV_W - 1, D_FF), dt)
    y_prompt, hg_p, C_p, n_p, m_p, cv_p = trunk(
        x_prompt, c_prompt, z_hg, z_C, z_n, z_m, z_cv, ada_w, ada_b, w_in, hg_lb_logits, hg_norm_w,
        ml_i_bias, ml_f_bias, ml_norm_w, w_out, conv_w, conv_b, w_up, w_down, final_norm_w)
    y_sample, hg_s, C_s, n_s, m_s, cv_s = trunk(
        x_sample, c_sample, state_hgrn, state_mlstm_C, state_mlstm_n, state_mlstm_m, state_conv, ada_w, ada_b,
        w_in, hg_lb_logits, hg_norm_w, ml_i_bias, ml_f_bias, ml_norm_w, w_out, conv_w, conv_b, w_up, w_down,
        final_norm_w)
    return (y_prompt, y_sample, hg_p, hg_s, C_p, C_s, n_p, n_s, m_p, m_s, cv_p, cv_s)


_drawn_inputs = setup_inputs


def setup_inputs(seed=0):
    import zlib

    import numpy as np

    out = dict(_drawn_inputs(seed))
    spreads = {}
    factors = {'hg_norm_w': 8.0, 'ml_norm_w': 8.0, 'conv_b': 8.0, 'final_norm_w': 2.829}
    for name, (base, spread) in spreads.items():
        noise = np.random.default_rng([zlib.crc32(name.encode()), seed]).standard_normal(out[name].shape)
        drawn = base * np.exp(spread * noise) if base else spread * noise
        out[name] = __import__('jax').numpy.asarray(drawn.astype(out[name].dtype))
    for name, factor in factors.items():
        out[name] = (out[name] * factor).astype(out[name].dtype)
    return out
```

```python
from contextlib import ExitStack

import numpy as np

import concourse.bass as bass
from concourse import mybir

F32 = mybir.dt.float32
F32R = mybir.dt.float32r
I32 = mybir.dt.int32
ALU = mybir.AluOpType
ACT = mybir.ActivationFunctionType

P = 128
D = 2048
KT = D // P
TP = 256
NS = 8
LS = 4
TS = NS * LS
T = TP + TS
NB = 1 + NS
NBP = NB + 1
EPS = 1e-6
HH = 16
MH = 8
MV = 256
FF = 5632
FT = FF // P
CW = 3
SUB = 32
NSUB = TP // SUB
HSC = float(P) ** -0.5
NEG = -1.0e30
ROW_WK = 16
ROW_T = ROW_WK
CONST_ALL = 28
FREE = 1
LEAD = 3
RING = 4
KC = 4
CN = 256

C_HQ, C_HF, C_HI, C_HG = 0, 2048, 4096, 6144
C_MQ, C_MK, C_MV, C_MI, C_MF, C_MO = 8192, 9216, 10240, 12288, 12296, 12304
C_GA, C_GB = 14352, 16400

HG_STEP = 40
ML_STEP = 32
S_ADA1 = 0
S_HG = S_ADA1 + 64
S_ML = S_HG + 4 * HG_STEP
S_ADA2 = S_ML + 4 * ML_STEP
S_OUT = S_ADA2 + 128
S_UP = S_OUT + 32
S_DOWN = S_UP + 22 * 8
S_END = S_DOWN + 88
Q_ADA1 = 0
Q_HG = Q_ADA1 + 8
Q_ML = Q_HG + 4 * 5
Q_ADA2 = Q_ML + 4 * 4
Q_OUT = Q_ADA2 + 16
Q_UP = Q_OUT + 4
Q_DOWN = Q_UP + 22

HG_NSTEP = 10
ML_NSTEP = 12


def steps_at(k, window, nsteps, heads):
    return [(j, o) for j in range(heads) for o in range(nsteps) if j * window + o * window // nsteps == k]


def build(nc, x_prompt, x_sample, c_prompt, c_sample, state_hgrn, state_mlstm_C, state_mlstm_n, state_mlstm_m,
          state_conv, ada_w, ada_b, w_in, hg_lb_logits, hg_norm_w, ml_i_bias, ml_f_bias, ml_norm_w, w_out,
          conv_w, conv_b, w_up, w_down, final_norm_w,
          y_prompt, y_sample, hg_p, hg_s, C_p, C_s, n_p, n_s, m_p, m_s, cv_p, cv_s):
    xT_spill = nc.dram_tensor("xT_spill", (P, KT * T), F32).ap()
    x1_spill = nc.dram_tensor("x1_spill", (P, KT * T), F32).ap()
    with ExitStack() as ctx:
        def sb(name, shape, dt=F32, stack=ctx):
            return stack.enter_context(nc.sbuf_tensor(name, shape, dt))

        def sem(name):
            return ctx.enter_context(nc.semaphore(name))

        raw = sb("raw", [P, RING, KC, CN])
        whi = sb("whi", [P, RING, KC, CN], F32R)
        wlo = sb("wlo", [P, RING, KC, CN], F32R)
        split = ExitStack()
        xh = sb("xh", [P, KT, T], F32R, stack=split)
        xl = sb("xl", [P, KT, T], F32R, stack=split)
        split.close()
        dno = sb("dno", [P, KT, T])
        x1f = sb("x1f", [P, KT, T])
        ch = sb("ch", [P, KT, NBP], F32R)
        cl = sb("cl", [P, KT, NBP], F32R)
        mod = sb("mod", [P, 6 * KT, NB])
        par = sb("par", [P, 4, P])
        cst = sb("cst", [P, FT, NS * 2])
        ident = sb("ident", [P, P])
        ones = sb("ones", [P, P])
        epsc = sb("epsc", [P, 1])
        onec = sb("onec", [P, 1])
        rstd = sb("rstd", [P, T])
        lnms = sb("lnms", [P, T])

        setup = ExitStack()
        mixer = ExitStack()
        ffn = ExitStack()
        merged = sb("merged", [P, KT, T], stack=mixer)
        lbc = sb("lbc", [P, 2, HH], stack=mixer)
        lbt = sb("lbt", [P, 2, HH], stack=mixer)
        hmask = sb("hmask", [P, P], I32, stack=mixer)
        hmask_s = sb("hmask_s", [TS, TS], I32, stack=mixer)
        maskf = sb("maskf", [P, P], stack=mixer)
        maskf_s = sb("maskf_s", [TS, TS], stack=mixer)
        reset = sb("reset", [P, T], stack=mixer)
        amask = sb("amask", [P, TP], stack=mixer)
        amask_s = sb("amask_s", [TS, TS], stack=mixer)
        bmask = sb("bmask", [TS, NS], stack=mixer)
        ones8 = sb("ones8", [MH, P], stack=mixer)
        acol = sb("acol", [P, 3, MH], stack=mixer)
        wkcol = sb("wkcol", [P, 3, MH], stack=mixer)
        LR = sb("LR", [MH, 2 * T + TS + NS], stack=mixer)
        nnew = sb("nnew", [P, NB, MH], stack=mixer)
        ntok = sb("ntok", [NB * MH, P], stack=mixer)
        LRW = 2 * T + TS + NS
        xT = sb("xT", [P, KT, T], stack=setup)
        xtm = sb("xtm", [P, 3, D], stack=setup)
        ctm = sb("ctm", [NB, D], stack=setup)
        cvr = sb("cvr", [NS * 2, FF], stack=setup)
        partm = sb("partm", [P, 4, P], stack=setup)
        gw = sb("gw", [P, KT, 2 * MH], stack=setup)
        gwh = sb("gwh", [P, KT, 2 * MH], F32R, stack=setup)
        gwl = sb("gwl", [P, KT, 2 * MH], F32R, stack=setup)
        gb = sb("gb", [MH, 2], stack=setup)
        m0 = sb("m0", [MH, NS], stack=setup)
        reset8 = sb("reset8", [MH, 2, T], stack=setup)
        setup.close()
        hg_mem = ExitStack()
        S = sb("S", [P, 5, 4, T], stack=hg_mem)
        W = sb("W", [P, 5, 4, T], stack=hg_mem)
        lf = sb("lf", [P, T], stack=hg_mem)
        bc = sb("bc", [P, T], stack=hg_mem)
        bm = sb("bm", [P, T], stack=hg_mem)
        e1 = sb("e1", [P, T], stack=hg_mem)
        e2 = sb("e2", [P, T], stack=hg_mem)
        er = sb("er", [P, NSUB], stack=hg_mem)
        dec = sb("dec", [P, NSUB], stack=hg_mem)
        qt = sb("qt", [P, T], stack=hg_mem)
        kt_ = sb("kt_", [P, T], stack=hg_mem)
        kh = sb("kh", [P, T], stack=hg_mem)
        qs = sb("qs", [P, TP], stack=hg_mem)
        PT = sb("PT", [P, 2, P], stack=hg_mem)
        PTs = sb("PTs", [TS, TS], stack=hg_mem)
        Vt = sb("Vt", [P, 2, P], stack=hg_mem)
        Vts = sb("Vts", [TS, P], stack=hg_mem)
        Kt = sb("Kt", [P, 2, P], stack=hg_mem)
        Kts = sb("Kts", [TS, P], stack=hg_mem)
        Vx = sb("Vx", [P, 2, 4, P], stack=hg_mem)
        Vxs = sb("Vxs", [TS, NS, P], stack=hg_mem)
        Sst = sb("Sst", [P, NSUB, P], stack=hg_mem)
        S0 = sb("S0", [P, NS, P], stack=hg_mem)
        hg_mem.close()
        ml_mem = ExitStack()
        mS = sb("mS", [P, 5 * 4, T], stack=ml_mem)
        mW = sb("mW", [P, 12, T], stack=ml_mem)
        mLR = sb("mLR", [MH, LRW], stack=ml_mem)
        em = sb("em", [P, T], stack=ml_mem)
        es = sb("es", [P, TS + NS], stack=ml_mem)
        arg = sb("arg", [P, 3 * P + TS], stack=ml_mem)
        dx = sb("dx", [P, 3 * P + TS], stack=ml_mem)
        pm = sb("pm", [P, 3 * P + TS], stack=ml_mem)
        qi = sb("qi", [P, TS], stack=ml_mem)
        qn = sb("qn", [P, TS], stack=ml_mem)
        mK = sb("mK", [P, 3, P], stack=ml_mem)
        mV = sb("mV", [P, 3, MV], stack=ml_mem)
        mVx = sb("mVx", [TS, NS, MV], stack=ml_mem)
        C0 = sb("C0", [P, NS, MV], stack=ml_mem)
        Cp = sb("Cp", [P, MV], stack=ml_mem)
        ndec = sb("ndec", [P, NS], stack=ml_mem)
        dn = sb("dn", [P, T], stack=ml_mem)
        hh = sb("hh", [P, 2, T], stack=ml_mem)
        hsq = sb("hsq", [P, 2, T], stack=ml_mem)
        ml_mem.close()
        post = ExitStack()
        mixo = sb("mixo", [P, KT, T], stack=post)
        xT2 = sb("xT2", [P, KT, T], stack=post)
        sqacc = sb("sqacc", [P, 4, T], stack=post)
        post.close()
        mixer.close()
        ffh = sb("ffh", [P, FT, T], F32R, stack=ffn)
        ffl = sb("ffl", [P, FT, T], F32R, stack=ffn)
        tails = sb("tails", [P, FT, 2 + NS * 2], stack=ffn)
        AB = 2 + TP + NS * (2 + LS)
        up = ExitStack()
        abuf = sb("abuf", [P, 2, AB], stack=up)
        acv = sb("acv", [P, 2, AB], stack=up)
        yb = sb("yb", [P, 2, T], stack=up)
        up.close()
        cts = sb("cts", [2 + NS * 2, 2, 512], stack=ffn)
        sqd = sb("sqd", [P, 2, T], stack=ffn)
        sqf = sb("sqf", [P, 2, T], stack=ffn)
        ffn.close()
        last = ExitStack()
        yT = sb("yT", [P, KT, T], stack=last)
        ytm = sb("ytm", [P, 3, D], stack=last)
        last.close()
        ps = ctx.enter_context(nc.psum_tensor("ps", [P, 2, 2, 512], F32))
        R = ctx.enter_context(nc.psum_tensor("R", [P, 4, 512], F32))
        Rf = R[:].rearrange("p a b -> p (a b)")

        landed = [sem(f"landed{i}") for i in range(RING)]
        hi_done = sem("hi_done")
        lo_done = sem("lo_done")
        used = sem("used")
        bank_free = [sem("bank_free0"), sem("bank_free1")]
        ld_c, ld_x, ld_par, ld_conv, ld_gw, ld_gs = (sem(n) for n in ("ld_c", "ld_x", "ld_par", "ld_conv", "ld_gw", "ld_gs"))
        const = sem("const")
        par_t, par_c = sem("par_t"), sem("par_c")
        c_silu, c_t, c_hi, c_lo, c_zero = (sem(n) for n in ("c_silu", "c_t", "c_hi", "c_lo", "c_zero"))
        cv_t, cv_c = sem("cv_t"), sem("cv_c")
        x_t, x_c = sem("x_t"), sem("x_c")
        sq_done, ms_done, rs_done, xn_done = (sem(n) for n in ("sq_done", "ms_done", "rs_done", "xn_done"))
        sc_one, md_p, md_s, xhi, xlo = (sem(n) for n in ("sc_one", "md_p", "md_s", "xhi", "xlo"))
        spill_x, back_x, spill_1, back_1 = (sem(n) for n in ("spill_x", "back_x", "spill_1", "back_1"))
        lb_a, lb_d = sem("lb_a"), sem("lb_d")
        gw_hi, gw_lo, gmm, row_a, row_d, row_t, row_c = (sem(n) for n in ("gw_hi", "gw_lo", "gmm", "row_a", "row_d", "row_t", "row_c"))
        st_m, st_n, st_y, st_cv = sem("st_m"), sem("st_n"), sem("st_y"), [sem("st_cv0"), sem("st_cv1")]
        hg = {n: sem("hg_" + n) for n in ("zero", "sig", "pre", "logf", "b", "bm", "exp", "qk", "dk", "scores", "tr", "pt",
                                          "tok", "vx", "u", "state", "o", "us", "sq", "scaled", "snew", "ms", "rstd",
                                          "y", "out", "s0", "st", "stored")}
        ml = {n: sem("ml_" + n) for n in ("sig", "pre", "lr", "bc", "qk", "kT", "e", "k", "arg", "d", "p", "q", "vT", "v",
                                          "vx", "num", "dn", "h", "cs", "sq", "ms", "st1", "st2", "r", "y", "c", "c2",
                                          "out", "c0", "st", "stored")}
        n_t, n_c = sem("n_t"), sem("n_c")
        x1_m, x1_a, x1_sq, x1_acc = (sem(n) for n in ("x1_m", "x1_a", "x1_sq", "x1_acc"))
        ab_ready, ab_lead, ab_tail = sem("ab_ready"), sem("ab_lead"), sem("ab_tail")
        ff_conv, ff_gelu, ff_y, ff_hi, ff_lo = (sem(n) for n in ("ff_conv", "ff_gelu", "ff_y", "ff_hi", "ff_lo"))
        tl_t, tl_c = sem("tl_t"), sem("tl_c")
        x2_m, x2_a, x2_sq, x2_acc = (sem(n) for n in ("x2_m", "x2_a", "x2_sq", "x2_acc"))
        y_w, y_t, y_c = sem("y_w"), sem("y_t"), sem("y_c")
        zab = sem("zab")

        ada_v = ada_w[0].rearrange("(kt p) n -> p kt n", p=P)
        win_v = w_in[0].rearrange("(kt p) n -> p kt n", p=P)
        out_v = w_out[0].rearrange("(kt p) n -> p kt n", p=P)
        up_v = w_up[0].rearrange("(kt p) n -> p kt n", p=P)
        down_v = w_down[0].rearrange("(kt p) n -> p kt n", p=P)

        def known(eng, x):
            if not isinstance(x, int):
                eng.compute_val(x)
            return x

        def mid(a, n):
            return a.rearrange("p (a m) -> p a m", a=1).to_broadcast([a.shape[0], n, a.shape[1]])

        def rep_last(a, n):
            return a.rearrange("p (m a) -> p m a", a=1).to_broadcast([a.shape[0], a.shape[1], n])

        def rep3(a, n):
            return a.rearrange("p k (m a) -> p k m a", a=1).to_broadcast([a.shape[0], a.shape[1], a.shape[2], n])

        def seq(a, n):
            return a.rearrange("p (c t) -> p c t", t=n)

        def seq3(a, n):
            return a.rearrange("p k (c t) -> p k c t", t=n)

        def hg_cols(i):
            return [c + 512 * i + 256 * u for c in (C_HQ, C_HF, C_HI, C_HG, C_GA) for u in range(2)]

        def ml_cols(i):
            return [C_MQ + 256 * i, C_MK + 256 * i] + [c + 512 * i + 256 * u for c in (C_MV, C_MO, C_GB) for u in range(2)]

        HG_AT = [steps_at(k, 10, HG_NSTEP, 4) for k in range(HG_STEP)]
        HG_AT_ML = [steps_at(k, 8, HG_NSTEP, 4) for k in range(ML_STEP)]
        ML_AT = [steps_at(k, 16, ML_NSTEP, 2) for k in range(ML_STEP)]
        bias_row = par[:, 0, :]
        gates_cols = (slice(0, TP), slice(TP, T))

        block = ctx.enter_context(nc.Block())

        @block.sync
        def _(sp):
            def load(c, k, src):
                if not isinstance(c, int) or c > RING - 1:
                    sp.wait_ge(lo_done, c - (RING - 1))
                sp.dma_start(raw[:, k % RING], src).then_inc(landed[k % RING], 16)

            def block256(c, k0, view, col, chunks=4, kt0=0):
                for s in range(chunks):
                    load(c + s, k0 + s, view[:, KC * (kt0 + s):KC * (kt0 + s + 1), bass.ds(col, CN)])

            def ada(C, col):
                for u in range(2):
                    block256(C + 4 * u, 4 * u, ada_v, col + CN * u)

            ada(S_ADA1, 0)
            with sp.Fori(1, 8) as i:
                ada(S_ADA1 + 8 * i, 512 * i)

            def hg_stream(C, i):
                for u, col in enumerate(hg_cols(i)):
                    block256(C + 4 * u, 4 * u, win_v, col)

            def ml_stream(C, i):
                for u, col in enumerate(ml_cols(i)):
                    block256(C + 4 * u, 4 * u, win_v, col)

            with sp.Fori(0, 4) as i:
                hg_stream(S_HG + HG_STEP * i, i)
            with sp.Fori(0, 4) as i:
                ml_stream(S_ML + ML_STEP * i, i)
            with sp.Fori(0, 16) as i:
                ada(S_ADA2 + 8 * i, 4096 + 512 * i)
            with sp.Fori(0, 4) as i:
                for u in range(2):
                    block256(S_OUT + 8 * i + 4 * u, 4 * u, out_v, 512 * i + CN * u)
            with sp.Fori(0, 22) as i:
                for u in range(2):
                    block256(S_UP + 8 * i + 4 * u, 4 * u, up_v, FF * u + CN * i)
            with sp.Fori(0, 2) as i:
                for u in range(4):
                    block256(S_DOWN + 44 * i + 11 * u, 11 * u, down_v, 1024 * i + CN * u, chunks=11)
            for tt in range(3):
                sp.wait_ge(y_c, 4 * (tt + 1))
                if tt < 2:
                    sp.dma_start(y_prompt[0, P * tt:P * (tt + 1), :], ytm[:, tt, :]).then_inc(st_y, 16)
                else:
                    sp.dma_start(y_sample.rearrange("b t d -> (b t) d"), ytm[0:TS, 2, :]).then_inc(st_y, 16)
            sp.wait_ge(st_y, 48)
            sp.wait_ge(st_m, 32)
            sp.wait_ge(st_n, 32)
            sp.wait_ge(st_cv[0], 32 * 6)
            sp.wait_ge(st_cv[1], 32 * 5)
            sp.wait_ge(hg["st"], 32 * HH)
            sp.wait_ge(ml["st"], 32 * MH)
            sp.wait_ge(spill_x, 16)
            sp.wait_ge(spill_1, 16)

        @block.tensor
        def _(pe):
            mm = nc.tensor.matmul

            def tr(out, in_):
                return nc.tensor.transpose(out, in_, ident[0:in_.shape[0], 0:in_.shape[0]])

            def chunk(c, k, first, last, bank, n, hi, lo, kt0):
                pe.wait_ge(lo_done, c + 1)
                s = k % RING
                for kk in range(KC):
                    for m in range(2):
                        cols = slice(P * m, P * (m + 1))
                        o = ps[:, bank, m, 0:n]
                        mm(o, whi[:, s, kk, cols], hi[:, kt0 + kk, :], start=first and kk == 0, stop=False)
                        mm(o, whi[:, s, kk, cols], lo[:, kt0 + kk, :], start=False, stop=False)
                        x = mm(o, wlo[:, s, kk, cols], hi[:, kt0 + kk, :], start=False, stop=last and kk == KC - 1)
                x.then_inc(used, 1)

            def stream(C, blocks, q, n, hi, lo, hook=None, xwait=None, chunks=4):
                for b in range(blocks):
                    pe.wait_ge(bank_free[b % 2], q + b // 2 + FREE)
                    for s in range(chunks):
                        k = chunks * b + s
                        if xwait is not None and b == 0:
                            pe.wait_ge(xlo, xwait + s + 1)
                        chunk(C + k, k, s == 0, s == chunks - 1, b % 2, n, hi, lo, KC * s)
                        if hook is not None:
                            hook(k)

            pe.sem_inc(used, FREE)
            pe.sem_inc(ml["bc"], FREE)
            pe.wait_ge(const, 4)
            pe.wait_ge(ld_c, 32)
            pe.wait_ge(c_silu, 1)
            for kt in range(KT):
                x = tr(R[:, 3, NB * kt:NB * (kt + 1)], ctm[0:NB, P * kt:P * (kt + 1)])
            x.then_inc(c_t, 1)
            pe.wait_ge(ld_par, 16 * 9)
            for t, r in enumerate((128, 92, 88, 108)):
                x = tr(R[:, 2, P * t:P * t + r], partm[0:r, t, :])
            x.then_inc(par_t, 1)
            pe.wait_ge(ld_x, 48)
            for kt in range(KT):
                if kt >= 2:
                    pe.wait_ge(x_c, kt - 1)
                for tt in range(3):
                    w = P if tt < 2 else TS
                    x = tr(R[:, kt % 2, P * tt:P * tt + w], xtm[0:w, tt, P * kt:P * (kt + 1)])
                x.then_inc(x_t, 1)
            pe.wait_ge(ld_conv, 16)
            for g in range(2):
                if g == 0:
                    pe.wait_ge(par_c, 1)
                    pe.wait_ge(c_lo, 1)
                for ft in range(22 * g, 22 * g + 22):
                    x = tr(R[:, 2 + g, 16 * (ft - 22 * g):16 * (ft - 22 * g) + 16], cvr[:, P * ft:P * (ft + 1)])
                x.then_inc(cv_t, 1)
            for kt in range(KT):
                pe.wait_ge(sq_done, kt + 1)
                if kt == 0:
                    pe.wait_ge(x_c, KT)
                x = mm(R[:, 0, 0:T], ones[:, :], merged[:, kt, :], start=kt == 0, stop=kt == KT - 1)
            x.then_inc(ms_done, 1)

            pe.wait_ge(c_lo, 1)
            with pe.Fori(0, 8) as i:
                stream(S_ADA1 + 8 * i, 2, Q_ADA1 + i, NBP, ch, cl)
            pe.wait_ge(gw_lo, 1)
            pe.wait_ge(rs_done, 2)
            for g in range(2):
                for kt in range(KT):
                    pe.wait_ge(xlo, kt // KC + 1)
                    cols = slice(MH * g, MH * (g + 1))
                    o = R[0:MH, g, 0:T]
                    mm(o, gwh[:, kt, cols], xh[:, kt, :], start=kt == 0, stop=False)
                    mm(o, gwh[:, kt, cols], xl[:, kt, :], start=False, stop=False)
                    x = mm(o, gwl[:, kt, cols], xh[:, kt, :], start=False, stop=kt == KT - 1)
            x.then_inc(gmm, 1)

            def hg_step(j, o, n):
                if o == 2:
                    pe.wait_ge(hg["qk"], 2 * (n + 1))
                    pe.wait_ge(hg["snew"], n + FREE)
                    for t in range(2):
                        x = mm(R[:, 0, P * t:P * (t + 1)], kt_[:, P * t:P * (t + 1)], qt[:, P * t:P * (t + 1)], start=True, stop=True)
                    x = mm(R[0:TS, 0, TP:T], kt_[:, TP:T], qt[:, TP:T], start=True, stop=True)
                    x.then_inc(hg["scores"], 1)
                    for dst, src, s in ((1, W[:, 2, j, :], 0), (2, kh, 1)):
                        if s:
                            pe.wait_ge(hg["dk"], 4 * (n + 1))
                            pe.wait_ge(hg["y"], n + FREE)
                        for t in range(2):
                            tr(R[:, dst, P * t:P * (t + 1)], src[:, P * t:P * (t + 1)])
                        tr(R[0:TS, dst, TP:TP + P], src[:, TP:T]).then_inc(hg["tr"], 1)
                if o == 4:
                    pe.wait_ge(hg["vx"], 5 * (n + 1))
                    pe.wait_ge(hg["rstd"], 2 * n + FREE)
                    for t, bank in ((0, 3), (1, 1)):
                        mm(R[:, bank, :], Kt[:, t, :], Vx[:, t].rearrange("p a b -> p (a b)"), start=True, stop=True).then_inc(hg["u"], 1)
                if o == 6:
                    pe.wait_ge(hg["pt"], 2 * (n + 1))
                    pe.wait_ge(hg["state"], 8 * (n + 1))
                    pe.wait_ge(hg["s0"], 16 * (n + 1))
                    for t in range(2):
                        mm(R[:, 2, P * t:P * (t + 1)], Vt[:, t, :], PT[:, t, :], start=t == 0, stop=False, skip_group_check=True)
                    for c in range(1, NSUB):
                        mm(R[:, 2, SUB * c:SUB * (c + 1)], Sst[:, c - 1, :], qs[:, SUB * c:SUB * (c + 1)], start=False, stop=False, skip_group_check=True)
                    mm(R[:, 2, TP:T], Vts[:, :], PTs[:, :], start=False, stop=False, skip_group_check=True)
                    for b in range(NS):
                        x = mm(R[:, 2, TP + LS * b:TP + LS * (b + 1)], S0[:, b, :], qt[:, TP + LS * b:TP + LS * (b + 1)], start=False, stop=b == NS - 1, skip_group_check=True)
                    x.then_inc(hg["o"], 1)
                    for u in range(2):
                        x = mm(R[:, u, :], Kts[:, :], Vxs[:, 4 * u:4 * u + 4, :].rearrange("p a b -> p (a b)"), start=True, stop=True)
                    x.then_inc(hg["us"], 1)
                if o == 8:
                    pe.wait_ge(hg["sq"], n + 1)
                    mm(R[:, 3, 0:T], ones[:, :], lf[:, :], start=True, stop=True).then_inc(hg["ms"], 1)

            def ml_step(j, o, n, i):
                q, k = mW[:, j, :], mW[:, 2 + j, :]
                if o == 1:
                    pe.wait_ge(ml["lr"], n + 1)
                    pe.wait_ge(ml["c2"], n + FREE)
                    pe.wait_ge(ml["c"], 4 * n + FREE)
                    mm(Rf[:, 0:512], ones8[:, :], mLR[:, 0:512], start=True, stop=True)
                    mm(Rf[:, 512:LRW], ones8[:, :], mLR[:, 512:LRW], start=True, stop=True).then_inc(ml["bc"], 1)
                    pe.wait_ge(ml["sig"], 4 * (i + 1))
                    mm(R[:, 2, 0:TP], k[:, 0:P], q[:, 0:TP], start=True, stop=True)
                    mm(R[:, 2, TP:TP + P], k[:, P:TP], q[:, P:TP], start=True, stop=True)
                    mm(R[0:TS, 2, 3 * P:3 * P + TS], k[:, TP:T], q[:, TP:T], start=True, stop=True).then_inc(ml["qk"], 1)
                    for t in range(2):
                        tr(R[:, 3, P * t:P * (t + 1)], k[:, P * t:P * (t + 1)])
                    tr(R[0:TS, 3, TP:TP + P], k[:, TP:T]).then_inc(ml["kT"], 1)
                if o == 4:
                    pe.wait_ge(ml["k"], 3 * (n + 1))
                    pe.wait_ge(ml["pre"], 2 * (i + 1))
                    for t in range(2):
                        for v in range(2):
                            tr(R[:, 3, MV * t + P * v:MV * t + P * (v + 1)], mW[:, 4 + 2 * j + v, P * t:P * (t + 1)])
                    pe.wait_ge(ml["arg"], 3 * (n + 1))
                    pe.wait_ge(ml["e"], 2 * (n + 1))
                    for v in range(2):
                        x = tr(R[0:TS, 0, P * v:P * (v + 1)], mW[:, 4 + 2 * j + v, TP:T])
                    x.then_inc(ml["vT"], 1)
                if o == 6:
                    pe.wait_ge(ml["v"], 2 * (n + 1))
                    pe.wait_ge(ml["p"], 2 * (n + 1))
                    pe.wait_ge(ml["q"], 2 * (n + 1))
                    pe.wait_ge(ml["c0"], 16 * (n + 1))
                    for v in range(3):
                        bank = 1 + v
                        lhs = [mV[:, 0, P * v:P * (v + 1)], mV[:, 1, P * v:P * (v + 1)], mV[0:TS, 2, P * v:P * (v + 1)]] if v < 2 else \
                            [ones[:, :], ones[:, :], ones[0:TS, :]]
                        mm(R[:, bank, 0:TP], lhs[0], pm[:, 0:TP], start=True, stop=False, skip_group_check=True)
                        mm(R[:, bank, P:TP], lhs[1], pm[:, TP:TP + P], start=False, stop=False, skip_group_check=True)
                        mm(R[:, bank, TP:T], lhs[2], pm[0:TS, 3 * P:3 * P + TS], start=False, stop=False, skip_group_check=True)
                        if v < 2:
                            for b in range(NS):
                                x = mm(R[:, bank, TP + LS * b:TP + LS * (b + 1)], C0[:, b, P * v:P * (v + 1)], qi[:, LS * b:LS * (b + 1)], start=False, stop=b == NS - 1, skip_group_check=True)
                        else:
                            x = mm(R[:, bank, TP:T], ones[:, :], qn[:, :], start=False, stop=True, skip_group_check=True)
                    x.then_inc(ml["num"], 1)
                if o == 8:
                    pe.wait_ge(ml["sq"], n + 1)
                    for v in range(2):
                        x = mm(R[:, 0, 0:T], ones[:, :], hsq[:, v, :], start=v == 0, stop=v == 1)
                    x.then_inc(ml["ms"], 1)
                    pe.wait_ge(ml["vx"], n + 1)
                    pe.wait_ge(ml["h"], 4 * (n + 1))
                    for t in range(2):
                        mm(R[:, 1, 0:MV], mK[:, t, :], mV[:, t, :], start=t == 0, stop=t == 1)
                    for t in range(2):
                        mm(R[:, 1, MV:MV + 1], mK[:, t, :], ones[:, 0:1], start=t == 0, stop=t == 1)
                    mm(R[:, 1, MV + 1:MV + 1 + NS], mK[0:TS, 2, :], bmask[:, :], start=True, stop=True)
                    for u in range(2):
                        x = mm(R[:, 2 + u, :], mK[0:TS, 2, :], mVx[:, 2 * u:2 * u + 2, :].rearrange("p a b -> p (a b)"), start=True, stop=True)
                    x.then_inc(ml["st1"], 1)
                if o == 10:
                    pe.wait_ge(ml["c"], 4 * (n + 1) + FREE)
                    for u in range(2):
                        x = mm(R[:, 2 + u, :], mK[0:TS, 2, :], mVx[:, 4 + 2 * u:6 + 2 * u, :].rearrange("p a b -> p (a b)"), start=True, stop=True)
                    x.then_inc(ml["st2"], 1)

            stream(S_HG, 10, Q_HG, T, xh, xl)
            pe.wait_ge(row_d, ROW_T)
            pe.wait_ge(row_a, 6)
            for g in range(2):
                for t in range(3):
                    w = P if t < 2 else TS
                    x = tr(R[0:w, 0, 32 * g + MH * t:32 * g + MH * (t + 1)], merged[0:MH, 8 + 5 * g, P * t:P * t + w])
            x.then_inc(row_t, 1)
            pe.wait_ge(row_c, 6)

            with pe.Fori(0, 3) as i:
                def hook(k):
                    for j, o in HG_AT[k]:
                        hg_step(j, o, 4 * i + j)
                stream(S_HG + HG_STEP + HG_STEP * i, 10, Q_HG + 5 + 5 * i, T, xh, xl, hook)

            def hook(k):
                for j, o in HG_AT_ML[k]:
                    hg_step(j, o, 12 + j)
            stream(S_ML, 8, Q_ML, T, xh, xl, hook)
            pe.wait_ge(hg["out"], HH + FREE)
            with pe.Fori(0, 3) as i:
                def hook(k):
                    for j, o in ML_AT[k]:
                        ml_step(j, o, 2 * i + j, i)
                stream(S_ML + ML_STEP + ML_STEP * i, 8, Q_ML + 4 + 4 * i, T, xh, xl, hook)

            def hook(k):
                for j, o in ML_AT[k]:
                    ml_step(j, o, 6 + j, 3)
            stream(S_ADA2, 8, Q_ADA2, NBP, ch, cl, hook)
            pe.wait_ge(ml["c"], 4 * MH + FREE)
            pe.wait_ge(ml["c2"], MH + FREE)
            nc.tensor.transpose(R[0:NB * MH, 1, 0:P], nnew[:].rearrange("p a b -> p (a b)"), ident[:, :]).then_inc(n_t, 1)
            with pe.Fori(0, 12) as i:
                stream(S_ADA2 + 32 + 8 * i, 2, Q_ADA2 + 4 + i, NBP, ch, cl)
            pe.wait_ge(xlo, 8)
            with pe.Fori(0, 4) as i:
                stream(S_OUT + 8 * i, 2, Q_OUT + i, T, xh, xl)
            pe.wait_ge(x1_acc, 4 + FREE)
            for t in range(4):
                x = mm(R[:, 0, 0:T], ones[:, :], sqacc[:, t, :], start=t == 0, stop=t == 3)
            x.then_inc(ms_done, 1)
            for s in range(KC):
                pe.wait_ge(xlo, 8 + s + 1)
            with pe.Fori(0, 22) as i:
                stream(S_UP + 8 * i, 2, Q_UP + i, T, xh, xl)

            def down(i, g0=None):
                for u in range(4):
                    pe.wait_ge(bank_free[u % 2], Q_DOWN + 2 * i + u // 2 + FREE)
                    for s in range(11):
                        k = 11 * u + s
                        if isinstance(i, int) and u == 0:
                            pe.wait_ge(ff_lo, 2 * (s + 1) + FREE)
                        chunk(S_DOWN + 44 * i + k, k, s == 0, s == 10, u % 2, T, ffh, ffl, KC * s)
                        if i == 0 and k % 2 == 0 and k < 22:
                            g = k // 2
                            pe.wait_ge(ab_tail, 44 + FREE)
                            if g >= 2:
                                pe.wait_ge(tl_c, g - 1)
                            for t in range(4):
                                x = tr(R[0:2 + NS * 2, 1 + g % 2, P * t:P * (t + 1)], tails[:, 4 * g + t, :])
                            x.then_inc(tl_t, 1)

            down(0)
            down(1)
            pe.wait_ge(x2_acc, 8)
            for t in range(2):
                x = mm(R[:, 0, 0:T], ones[:, :], sqf[:, t, :], start=t == 0, stop=t == 1)
            x.then_inc(ms_done, 1)
            for tt in range(3):
                w = P if tt < 2 else TS
                for g in range(4):
                    e = 4 * tt + g
                    pe.wait_ge(y_w, 4 * (g + 1))
                    if e < 3:
                        pe.wait_ge(tl_c, 11)
                    if e >= 3:
                        pe.wait_ge(y_c, e - 2)
                    for t in range(4):
                        x = tr(R[0:w, 1 + e % 3, P * t:P * (t + 1)], yT[:, 4 * g + t, P * tt:P * tt + w])
                    x.then_inc(y_t, 1)

        @block.scalar
        def _(act):
            A = nc.scalar.activation

            def hi(C, k):
                s = k % RING
                act.wait_ge(landed[s], C * 4 + 16 * (k // RING + 1))
                if not isinstance(C, int) or C + k >= RING:
                    act.wait_ge(used, C + k - (RING - 1) + FREE)
                A(whi[:, s], raw[:, s], ACT.Copy).then_inc(hi_done, 1)

            act.sem_inc(hg["rstd"], FREE)
            act.dma_start(ctm[0:1, :], c_prompt).then_inc(ld_c, 16)
            act.dma_start(ctm[1:NB, :], c_sample).then_inc(ld_c, 16)
            for t in range(2):
                act.dma_start(xtm[:, t, :], x_prompt[0, P * t:P * (t + 1), :]).then_inc(ld_x, 16)
            act.dma_start(xtm[0:TS, 2, :], x_sample.rearrange("b t d -> (b t) d")).then_inc(ld_x, 16)

            def row128(a):
                return a.rearrange("(r c) -> r c", c=P)
            for dst, src in ((partm[0:96, 0, :], row128(ada_b[0])),
                             (partm[96:128, 0, :], hg_lb_logits.rearrange("i (r c) -> (i r) c", c=P)),
                             (partm[0:16, 1, :], row128(hg_norm_w[0])), (partm[16:32, 1, :], row128(ml_norm_w[0])),
                             (partm[32:48, 1, :], row128(final_norm_w)), (partm[48:92, 1, :], row128(conv_b[0])),
                             (partm[0:88, 2, :], conv_w[0, 0:2].rearrange("j (r c) -> (j r) c", c=P)),
                             (partm[0:44, 3, :], row128(conv_w[0, 2])),
                             (partm[44:108, 3, :], state_mlstm_n[0].rearrange("b h d -> (b h) d"))):
                act.dma_start(dst, src).then_inc(ld_par, 16)
            with nc.allow_non_contiguous_dma(reason="a few columns"):
                act.dma_start(gw[:, :, :], win_v[:, :, C_MI:C_MI + 2 * MH]).then_inc(ld_gw, 16)
                act.dma_start(gb[:, 0:1], ml_i_bias.rearrange("a h -> h a")).then_inc(ld_gs, 16)
                act.dma_start(gb[:, 1:2], ml_f_bias.rearrange("a h -> h a")).then_inc(ld_gs, 16)
                act.dma_start(m0[:, :], state_mlstm_m[0].rearrange("b h -> h b")).then_inc(ld_gs, 16)
            act.dma_start(cvr[:, :], state_conv[0].rearrange("b j f -> (b j) f")).then_inc(ld_conv, 16)

            act.wait_ge(ld_c, 32)
            A(ctm[:, :], ctm[:, :], ACT.Silu).then_inc(c_silu, 1)
            act.wait_ge(c_zero, 2)
            act.wait_ge(c_t, 1)
            A(ch[:, :, 0:NB], R[:, 3, 0:KT * NB].rearrange("p (k b) -> p k b", b=NB), ACT.Copy).then_inc(c_hi, 1)
            act.wait_ge(par_t, 1)
            A(par[:, 0, :], R[:, 2, 0:P], ACT.Copy)
            A(par[:, 1, 0:92], R[:, 2, P:P + 92], ACT.Copy)
            A(par[:, 2, 0:88], R[:, 2, 2 * P:2 * P + 88], ACT.Copy)
            A(par[:, 3, 0:108], R[:, 2, 3 * P:3 * P + 108], ACT.Copy).then_inc(par_c, 1)
            for k in range(LEAD):
                hi(0, k)
            for kt in range(KT):
                act.wait_ge(x_t, kt + 1)
                A(xT[:, kt, :], R[:, kt % 2, 0:T], ACT.Copy).then_inc(x_c, 1)
                act.wait_ge(x_c, kt + 1)
                A(merged[:, kt, :], xT[:, kt, :], ACT.Square).then_inc(sq_done, 1)
            for g in range(2):
                act.wait_ge(cv_t, g + 1)
                A(cst[:, 22 * g:22 * g + 22, :], R[:, 2 + g, 0:352].rearrange("p (f r) -> p f r", r=16), ACT.Copy).then_inc(cv_c, 1)

            def root(nth, src, scale):
                act.wait_ge(ms_done, nth)
                if nth > 1:
                    act.wait_ge(xn_done, 4 * (nth - 1))
                A(lnms[:, :], src, ACT.Ln, bias=epsc[:, 0:1], scale=scale).then_inc(rs_done, 1)
                act.wait_ge(rs_done, 2 * nth - 1)
                A(rstd[:, :], lnms[:, :], ACT.Exp, scale=-0.5).then_inc(rs_done, 1)

            act.wait_ge(const, 6)
            root(1, R[:, 0, 0:T], 1.0 / D)
            act.wait_ge(lb_d, 3)
            A(lbc[:, :, :], lbc[:, :, :], ACT.Exp).then_inc(lb_a, 1)
            act.wait_ge(ld_gw, 16)
            A(gwh[:, :, :], gw[:, :, :], ACT.Copy).then_inc(gw_hi, 1)

            with act.Fori(0, 8) as i:
                for k in range(8):
                    hi(S_ADA1 + 8 * i, k + LEAD)

            def modulate(nth, tmp, shift, scale):
                act.wait_ge(sc_one, nth)
                for g in range(4):
                    act.wait_ge(xn_done, 4 * (nth - 1) + g + 1)
                    for kt in range(4 * g, 4 * g + 4):
                        x = A(tmp[:, kt, 0:TP], tmp[:, kt, 0:TP], ACT.Identity, bias=mod[:, shift + kt, 0:1], scale=mod[:, scale + kt, 0:1])
                    x.then_inc(md_p, 1)
                    act.wait_ge(md_p, 4 * (nth - 1) + g + 1)
                    act.wait_ge(md_s, 2 * (4 * (nth - 1) + g + 1))
                    if g == 0 and nth == 2:
                        act.wait_ge(used, S_UP + FREE)
                    A(xh[:, 4 * g:4 * g + 4, :], tmp[:, 4 * g:4 * g + 4, :], ACT.Copy).then_inc(xhi, 1)

            modulate(1, merged, 0, KT)
            r = merged[0:MH]
            act.wait_ge(gmm, 1)
            act.wait_ge(ld_gs, 48)
            act.wait_ge(xlo, 4)
            A(r[:, 0, :], R[0:MH, 0, 0:T], ACT.Identity, bias=gb[:, 0:1]).then_inc(row_a, 1)
            A(r[:, 1, :], R[0:MH, 1, 0:T], ACT.Identity, bias=gb[:, 1:2]).then_inc(row_a, 1)
            act.wait_ge(row_a, 2)
            A(r[:, 2, :], r[:, 1, :], ACT.Abs).then_inc(row_a, 1)
            act.wait_ge(row_a, 3)
            A(r[:, 3, :], r[:, 2, :], ACT.Exp, scale=-1.0).then_inc(row_a, 1)
            act.wait_ge(row_a, 4)
            A(r[:, 4, :], r[:, 3, :], ACT.Ln, bias=onec[0:MH, 0:1]).then_inc(row_a, 1)
            act.wait_ge(row_d, ROW_WK)
            A(r[:, 13, :], r[:, 12, :], ACT.Exp).then_inc(row_a, 1)

            def evac(dst, C, k, par_, n):
                act.wait_ge(used, C + k + 1 + FREE)
                A(dst, ps[:, par_, :, 0:n], ACT.Copy).then_inc(bank_free[par_], 1)

            def hg_stream(C, hook=None):
                for k in range(HG_STEP):
                    hi(C, k + LEAD)
                    if k % 4 == 3:
                        b = k // 4
                        evac(S[:, b // 2, 2 * (b % 2):2 * (b % 2) + 2, :], C, k, b % 2, T)
                    if hook is not None:
                        hook(k)

            def ml_stream(C, hook):
                for k in range(ML_STEP):
                    hi(C, k + LEAD)
                    if k % 4 == 3:
                        b = k // 4
                        evac(mS[:, 2 * b:2 * b + 2, :], C, k, b % 2, T)
                    hook(k)

            def hg_prologue(i):
                for p in range(2):
                    act.wait_ge(bank_free[p], Q_HG + 5 * (i + 1) + FREE)
                act.wait_ge(hg["out"], 4 * i + FREE)
                A(W[:, 1], S[:, 1], ACT.Sigmoid, scale=-1.0).then_inc(hg["sig"], 1)
                A(W[:, 0], S[:, 0], ACT.Sigmoid).then_inc(hg["sig"], 1)
                A(W[:, 3], S[:, 3], ACT.Sigmoid).then_inc(hg["sig"], 1)
                A(W[:, 4], S[:, 4], ACT.Sigmoid).then_inc(hg["sig"], 1)
                act.wait_ge(hg["pre"], 4 * (i + 1))

            def hg_step(j, o, n, i):
                h = n
                if o == 0:
                    act.wait_ge(hg["sig"], 4 * (i + 1))
                    A(lf[:, :], W[:, 1, j, :], ACT.Ln, bias=onec[:, 0:1], scale=lbc[:, 0, bass.ds(h, 1)]).then_inc(hg["logf"], 1)
                if o == 1:
                    act.wait_ge(hg["bm"], 2 * (n + 1))
                    act.wait_ge(hg["out"], n + FREE)
                    A(e1[:, :], bm[:, :], ACT.Exp).then_inc(hg["exp"], 1)
                    A(e2[:, :], bm[:, :], ACT.Exp, scale=-1.0).then_inc(hg["exp"], 1)
                    A(er[:, :], seq(bc[:, 0:TP], SUB)[:, :, SUB // 2 - 1], ACT.Exp).then_inc(hg["exp"], 1)
                if o == 3:
                    act.wait_ge(hg["tr"], 2 * (n + 1))
                    A(Vt[:, :, :], R[:, 1, 0:TP].rearrange("p (a b) -> p a b", a=2), ACT.Copy).then_inc(hg["tok"], 1)
                    A(Vts[:, :], R[0:TS, 1, TP:TP + P], ACT.Copy).then_inc(hg["tok"], 1)
                    A(Kt[:, :, :], R[:, 2, 0:TP].rearrange("p (a b) -> p a b", a=2), ACT.Copy).then_inc(hg["tok"], 1)
                    A(Kts[:, :], R[0:TS, 2, TP:TP + P], ACT.Copy).then_inc(hg["tok"], 1)
                if o == 7:
                    act.wait_ge(hg["o"], n + 1)
                    A(lf[:, :], R[:, 2, 0:T], ACT.Square).then_inc(hg["sq"], 1)
                if o == 8:
                    act.wait_ge(hg["ms"], n + 1)
                    A(bc[:, :], R[:, 3, 0:T], ACT.Ln, bias=epsc[:, 0:1], scale=1.0 / P).then_inc(hg["rstd"], 1)
                    act.wait_ge(hg["rstd"], 2 * n + 1 + FREE)
                    A(e2[:, :], bc[:, :], ACT.Exp, scale=-0.5).then_inc(hg["rstd"], 1)

            def ml_prologue(i):
                for p in range(2):
                    act.wait_ge(bank_free[p], Q_ML + 4 * (i + 1) + FREE)
                act.wait_ge(ml["out"], 4 * i + FREE)
                A(mW[:, 8:12, :], mS[:, 8:12, :], ACT.Sigmoid).then_inc(ml["sig"], 1)
                A(mS[:, 12:16, :], mS[:, 12:16, :], ACT.Sigmoid).then_inc(ml["sig"], 1)
                A(mW[:, 0:2, :], mS[:, 0:2, :], ACT.Copy, scale=HSC).then_inc(ml["sig"], 1)
                A(mW[:, 2:4, :], mS[:, 2:4, :], ACT.Copy).then_inc(ml["sig"], 1)
                act.wait_ge(ml["pre"], 2 * (i + 1))

            def ml_step(j, o, n, i):
                h = n
                if o == 2:

                    act.wait_ge(ml["kT"], n + 1)
                    for t in range(3):
                        w = P if t < 2 else TS
                        A(mK[0:w, t, :], R[0:w, 3, P * t:P * (t + 1)], ACT.Copy, scale=wkcol[0:w, t, bass.ds(h, 1)]).then_inc(ml["k"], 1)
                    act.wait_ge(ml["arg"], 3 * (n + 1))
                    A(em[:, :], Rf[:, T:2 * T], ACT.Exp).then_inc(ml["e"], 1)
                    A(es[:, :], Rf[:, 2 * T:LRW], ACT.Exp).then_inc(ml["e"], 1)
                if o == 3:
                    act.wait_ge(ml["arg"], 3 * (n + 1))
                    for t, (w, a, b) in enumerate(((P, 0, TP), (P, TP, 3 * P), (TS, 3 * P, 3 * P + TS))):
                        A(dx[0:w, a:b], arg[0:w, a:b], ACT.Exp, bias=acol[0:w, t, bass.ds(h, 1)]).then_inc(ml["d"], 1)
                if o == 5:
                    act.wait_ge(ml["vT"], n + 1)
                    A(mV[:, 0:2, :], R[:, 3, :].rearrange("p (a b) -> p a b", a=2), ACT.Copy).then_inc(ml["v"], 1)
                    A(mV[0:TS, 2, :], R[0:TS, 0, 0:MV], ACT.Copy).then_inc(ml["v"], 1)
                if o == 7:
                    act.wait_ge(ml["num"], n + 1)
                    A(dn[:, :], R[:, 3, 0:T], ACT.Abs).then_inc(ml["dn"], 1)
                if o == 8:
                    act.wait_ge(ml["h"], 4 * (n + 1))
                    A(hsq[:, :, :], hh[:, :, :], ACT.Square).then_inc(ml["sq"], 1)
                if o == 9:
                    act.wait_ge(ml["ms"], n + 1)
                    A(em[:, :], R[:, 0, 0:T], ACT.Ln, bias=epsc[:, 0:1], scale=1.0 / MV).then_inc(ml["r"], 1)
                    act.wait_ge(ml["r"], 2 * n + 1)
                    A(dn[:, :], em[:, :], ACT.Exp, scale=-0.5).then_inc(ml["r"], 1)

            act.wait_ge(spill_x, 16)
            hg_stream(S_HG)
            act.wait_ge(row_t, 1)
            for g, dst in ((0, acol), (1, wkcol)):
                for t in range(3):
                    w = P if t < 2 else TS
                    A(dst[0:w, t, :], R[0:w, 0, 32 * g + MH * t:32 * g + MH * (t + 1)], ACT.Copy).then_inc(row_c, 1)
            with act.Fori(0, 3) as i:
                def hook(k):
                    for j, o in HG_AT[k]:
                        hg_step(j, o, 4 * i + j, i)
                hg_prologue(i)
                hg_stream(S_HG + HG_STEP + HG_STEP * i, hook)

            def hook(k):
                for j, o in HG_AT_ML[k]:
                    hg_step(j, o, 12 + j, 3)
            hg_prologue(3)
            ml_stream(S_ML, hook)
            act.wait_ge(hg["out"], HH + FREE)
            with act.Fori(0, 3) as i:
                def hook(k):
                    for j, o in ML_AT[k]:
                        ml_step(j, o, 2 * i + j, i)
                ml_prologue(i)
                ml_stream(S_ML + ML_STEP + ML_STEP * i, hook)
            ml_prologue(3)
            for k in range(32):
                hi(S_ADA2, k + LEAD)
                for j, o in ML_AT[k]:
                    ml_step(j, o, 6 + j, 3)
            act.wait_ge(n_t, 1)
            A(ntok[:, :], R[0:NB * MH, 1, 0:P], ACT.Copy).then_inc(n_c, 1)
            act.wait_ge(ml["out"], 2 * MH + FREE)
            act.wait_ge(used, S_ADA2 + FREE)
            for g in range(4):
                A(xh[:, 4 * g:4 * g + 4, :], merged[:, 4 * g:4 * g + 4, :], ACT.Copy).then_inc(xhi, 1)
            with act.Fori(0, 12) as i:
                for k in range(8):
                    hi(S_ADA2 + 32 + 8 * i, k + LEAD)
            with act.Fori(0, 4) as i:
                for k in range(8):
                    hi(S_OUT + 8 * i, k + LEAD)
                act.wait_ge(x1_a, 2 * (i + 1))
                A(mixo[:, bass.ds(4 * i, 4), :], xT2[:, bass.ds(4 * i, 4), :], ACT.Square).then_inc(x1_sq, 1)
            root(2, R[:, 0, 0:T], 1.0 / D)
            modulate(2, mixo, 3 * KT, 4 * KT)
            act.wait_ge(spill_1, 16)
            with act.Fori(0, 22) as i:
                C = S_UP + 8 * i
                for k in range(8):
                    hi(C, k + LEAD)
                    if k == 3:
                        act.wait_ge(used, C + 4 + FREE)
                        act.wait_ge(ff_conv, 6 * i + FREE)
                        act.wait_ge(ab_tail, 2 * i + FREE)
                        A(abuf[:, :, 2:2 + TP], ps[:, 0, :, 0:TP], ACT.Copy).then_inc(ab_ready, 1)
                        A(seq3(abuf[:, :, 2 + TP:AB], 2 + LS)[:, :, :, 2:2 + LS], seq3(ps[:, 0, :, TP:T], LS), ACT.Copy).then_inc(bank_free[0], 1)
                    if k == 5:
                        act.wait_ge(ff_conv, 6 * (i + 1) + FREE)
                        A(acv[:, :, 0:AB - 2], acv[:, :, 0:AB - 2], ACT.Gelu).then_inc(ff_gelu, 1)
                    if k == 7:
                        act.wait_ge(bank_free[1], Q_UP + i + 1 + FREE)
                        A(ffh[:, bass.ds(2 * i, 2), :], yb[:, :, :], ACT.Copy).then_inc(ff_hi, 1)

            def down(i):
                for k in range(44):
                    if not isinstance(i, int) or S_DOWN + 44 * i + k + LEAD < S_END:
                        hi(S_DOWN + 44 * i, k + LEAD)
                    if i == 0 and k % 2 == 1 and k < 22:
                        g = k // 2
                        act.wait_ge(tl_t, g + 1)
                        if g >= 2:
                            act.wait_ge(st_cv[g % 2], 32 * (g // 2))
                        A(cts[:, g % 2, :], R[0:2 + NS * 2, 1 + g % 2, :], ACT.Copy).then_inc(tl_c, 1)
                    if k % 11 == 10:
                        b = 4 * i + k // 11
                        act.wait_ge(x2_a, b + 1)
                        if b >= 1:
                            act.wait_ge(x2_acc, b)
                        A(sqd[:, :, :], x1f[:, 2 * b:2 * b + 2, :], ACT.Square).then_inc(x2_sq, 1)
            down(0)
            down(1)
            root(3, R[:, 0, 0:T], 1.0 / D)
            for e in range(0, 12, 2):
                act.wait_ge(y_t, e + 1)
                if e:
                    act.wait_ge(y_c, e)
                w = P if e < 8 else TS
                A(ytm[0:w, e // 4, 512 * (e % 4):512 * (e % 4) + 512], R[0:w, 1 + e % 3, :], ACT.Copy).then_inc(y_c, 1)

        @block.vector
        def _(dve):
            TT, TSC, STT = nc.vector.tensor_tensor, nc.vector.tensor_scalar, nc.vector.scalar_tensor_tensor

            def lo(c, k):
                s = k % RING
                dve.wait_ge(hi_done, c + k + 1)
                TT(wlo[:, s], raw[:, s], whi[:, s].bitcast(F32), ALU.subtract).then_inc(lo_done, 1)

            nc.vector.memset(ch[:, :, :].bitcast(F32), 0.0).then_inc(c_zero, 1)
            nc.vector.memset(cl[:, :, :].bitcast(F32), 0.0).then_inc(c_zero, 1)
            dve.wait_ge(c_zero, 2)
            dve.wait_ge(c_hi, 1)
            TT(cl[:, :, 0:NB], R[:, 3, 0:KT * NB].rearrange("p (k b) -> p k b", b=NB), ch[:, :, 0:NB].bitcast(F32), ALU.subtract).then_inc(c_lo, 1)
            for s in (bank_free[0], bank_free[1], hg["snew"], hg["y"], ml["c"], ml["c2"], ff_conv, ff_lo):
                dve.sem_inc(s, FREE)
            for k in range(LEAD):
                lo(0, k)
            dve.wait_ge(par_c, 1)
            lg = par[:, 0, 96:128].rearrange("p (i h) -> p i h", i=2)
            TT(lbt[:, 0, :], lg[:, 0, :], lg[:, 1, :], ALU.max).then_inc(lb_d, 1)
            dve.wait_ge(lb_d, 1)
            TT(lbc[:, 0, :], lg[:, 0, :], lbt[:, 0, :], ALU.subtract).then_inc(lb_d, 1)
            TT(lbc[:, 1, :], lg[:, 1, :], lbt[:, 0, :], ALU.subtract).then_inc(lb_d, 1)
            dve.wait_ge(lb_a, 1)
            lsum, lrec = lbt[:, 0, :], lbt[:, 1, :]
            TT(lsum, lbc[:, 0, :], lbc[:, 1, :], ALU.add).then_inc(lb_d, 1)
            dve.wait_ge(lb_d, 4)
            nc.vector.reciprocal(lrec, lsum).then_inc(lb_d, 1)
            dve.wait_ge(lb_d, 5)
            TT(lsum, lbc[:, 0, :], lrec, ALU.mult).then_inc(lb_d, 1)
            dve.wait_ge(lb_d, 6)
            TSC(lbc[:, 0, :], lsum, 1.0, None, ALU.subtract).then_inc(lb_d, 1)
            TSC(lbc[:, 1, :], lsum, -1.0, 1.0, ALU.mult, ALU.add).then_inc(lb_d, 1)
            dve.wait_ge(gw_hi, 1)
            TT(gwl[:, :, :], gw[:, :, :], gwh[:, :, :].bitcast(F32), ALU.subtract).then_inc(gw_lo, 1)

            def ada(C, q, mt, hook=None):
                for k in range(8):
                    lo(C, k + LEAD)
                    if k % 4 == 3:
                        b = k // 4
                        dve.wait_ge(used, C + k + 1 + FREE)
                        TT(mod[:, bass.ds(mt + 2 * b, 2), :], ps[:, b, :, 0:NB], rep_last(bias_row[:, bass.ds(mt + 2 * b, 2)], NB), ALU.add).then_inc(bank_free[b], 1)

            with dve.Fori(0, 8) as i:
                ada(S_ADA1 + 8 * i, i, 4 * i)

            def modulate(nth, src, tmp, shift, scale):
                dve.wait_ge(rs_done, 2 * nth)
                for p in range(2):
                    dve.wait_ge(bank_free[p], (Q_HG if nth == 1 else Q_OUT) + FREE)
                TSC(mod[:, scale:scale + KT, :], mod[:, scale:scale + KT, :], 1.0, None, ALU.add).then_inc(sc_one, 1)
                dve.wait_ge(sc_one, nth)
                for g in range(4):
                    a, b = 4 * g, 4 * g + 4
                    m = 4 * (nth - 1) + g
                    TT(tmp[:, a:b, :], src[:, a:b, :], mid(rstd[:, :], 4), ALU.mult).then_inc(xn_done, 1)
                    dve.wait_ge(xn_done, m + 1)
                    v = seq3(tmp[:, a:b, TP:T], LS)
                    TT(v, v, rep3(mod[:, scale + a:scale + b, 1:NB], LS), ALU.mult).then_inc(md_s, 1)
                    dve.wait_ge(md_s, 2 * m + 1)
                    TT(v, v, rep3(mod[:, shift + a:shift + b, 1:NB], LS), ALU.add).then_inc(md_s, 1)
                for g in range(4):
                    a, b = 4 * g, 4 * g + 4
                    dve.wait_ge(xhi, 4 * (nth - 1 if nth == 1 else 2) + g + 1)
                    TT(xl[:, a:b, :], tmp[:, a:b, :], xh[:, a:b, :].bitcast(F32), ALU.subtract).then_inc(xlo, 1)

            modulate(1, xT, merged, 0, KT)
            r = merged[0:MH]
            cnt = [0]

            def row(ins):
                cnt[0] += 1
                ins.then_inc(row_d, 1)
                dve.wait_ge(row_d, cnt[0])
            dve.wait_ge(row_a, 5)
            dve.wait_ge(const, CONST_ALL)
            row(TSC(r[:, 5, :], r[:, 1, :], 0.0, None, ALU.min))
            row(TT(r[:, 6, :], r[:, 5, :], r[:, 4, :], ALU.subtract))
            row(nc.vector.tensor_tensor_scan(r[:, 7, :], reset8[:, 0, :], r[:, 6, :], 0.0, ALU.mult, ALU.add))
            row(TT(r[:, 8, :], r[:, 0, :], r[:, 7, :], ALU.subtract))
            row(nc.vector.tensor_copy(r[:, 9, :], r[:, 8, :]))
            row(TSC(r[:, 9, 0:1], r[:, 8, 0:1], 0.0, None, ALU.max))
            row(TT(seq(r[:, 9, TP:T], LS)[:, :, 0], seq(r[:, 8, TP:T], LS)[:, :, 0], m0[:, :], ALU.max))
            row(nc.vector.tensor_tensor_scan(r[:, 10, :], reset8[:, 1, :], r[:, 9, :], 0.0, ALU.add, ALU.max))
            row(TSC(LR[:, 0:T], r[:, 10, :], -1.0, None, ALU.mult))
            row(TT(LR[:, T:2 * T], LR[:, 0:T], r[:, 7, :], ALU.subtract))
            nM = seq(LR[:, TP:T], LS)
            row(TT(seq(LR[:, 2 * T:2 * T + TS], LS), nM, rep_last(m0[:, :], LS), ALU.add))
            row(TT(LR[:, 2 * T + TS:LRW], nM[:, :, LS - 1], m0[:, :], ALU.add))
            row(TSC(r[:, 11, 0:1], LR[:, T + TP - 1:T + TP], -1.0, None, ALU.mult))
            row(TSC(r[:, 11, 1:NB], seq(LR[:, T + TP:2 * T], LS)[:, :, LS - 1], -1.0, None, ALU.mult))
            row(TSC(r[:, 12, 0:TP], r[:, 8, 0:TP], LR[:, TP - 1:TP], None, ALU.add))
            row(TT(seq(r[:, 12, TP:T], LS), seq(r[:, 8, TP:T], LS), nM[:, :, LS - 1:LS].to_broadcast([MH, NS, LS]), ALU.add))
            assert cnt[0] == ROW_WK == ROW_T

            def hg_step(j, o, n, i):
                h = n
                if o == 0:
                    dve.wait_ge(hg["logf"], n + 1)
                    dve.wait_ge(lb_d, 8)
                    nc.vector.tensor_tensor_scan(bc[:, :], reset[:, :], lf[:, :], 0.0, ALU.mult, ALU.add).then_inc(hg["b"], 1)
                    dve.wait_ge(hg["b"], n + 1)
                    v = seq(bc[:, 0:TP], SUB)
                    TT(seq(bm[:, 0:TP], SUB), v, v[:, :, SUB // 2 - 1:SUB // 2].to_broadcast([P, NSUB, SUB]), ALU.subtract).then_inc(hg["bm"], 1)
                    nc.vector.tensor_copy(bm[:, TP:T], bc[:, TP:T]).then_inc(hg["bm"], 1)
                if o == 1:
                    dve.wait_ge(hg["exp"], 3 * (n + 1))
                    dve.wait_ge(hg["pre"], 4 * (i + 1))
                    STT(qt[:, :], W[:, 0, j, :], HSC, e1[:, :], ALU.mult, ALU.mult).then_inc(hg["qk"], 1)
                    STT(kt_[:, :], W[:, 1, j, :], lbc[:, 1, bass.ds(h, 1)], e2[:, :], ALU.mult, ALU.mult).then_inc(hg["qk"], 1)
                if o == 3:
                    count = known(dve, n + 1)
                    dve.wait_ge(const, CONST_ALL)
                    dve.wait_ge(hg["scores"], count)
                    nc.vector.copy_predicated(PT[:, :, :], mid(hmask[:, :], 2), R[:, 0, 0:TP].rearrange("p (a b) -> p a b", a=2)).then_inc(hg["pt"], 1)
                    nc.vector.copy_predicated(PTs[:, :], hmask_s[:, :], R[0:TS, 0, TP:T]).then_inc(hg["pt"], 1)
                if o == 5:
                    dve.wait_ge(hg["u"], 2 * (n + 1))
                    dve.wait_ge(hg["dk"], 4 * (n + 1))
                    dve.wait_ge(hg["stored"], n + FREE)
                    nc.vector.tensor_copy(Sst[:, 0, :], R[:, 3, 0:P]).then_inc(hg["state"], 1)
                    for c in range(1, NSUB):
                        dve.wait_ge(hg["state"], 8 * n + c)
                        STT(Sst[:, c, :], Sst[:, c - 1, :], dec[:, c:c + 1], R[:, 3 if c < 4 else 1, P * (c % 4):P * (c % 4 + 1)], ALU.mult, ALU.add).then_inc(hg["state"], 1)
                if o == 7:
                    dve.wait_ge(hg["us"], n + 1)
                    dve.wait_ge(hg["scaled"], n + 1)
                    TT(S0[:].rearrange("p a b -> p (a b)"), S0[:].rearrange("p a b -> p (a b)"), Rf[:, 0:1024], ALU.add).then_inc(hg["snew"], 1)
                if o == 8:
                    dve.wait_ge(hg["rstd"], 2 * (n + 1) + FREE)
                    STT(e1[:, :], R[:, 2, 0:T], par[:, 1, bass.ds(h, 1)], e2[:, :], ALU.mult, ALU.mult).then_inc(hg["y"], 1)

            def ml_step(j, o, n, i):
                h = n
                if o == 0:
                    dve.wait_ge(ml["bc"], n + FREE)
                    TSC(mLR[:, :], LR[:, :], ident[0:MH, bass.ds(h, 1)], None, ALU.mult).then_inc(ml["lr"], 1)
                if o == 2:
                    dve.wait_ge(ml["bc"], n + 1 + FREE)
                    TT(arg[:, 0:TP], R[:, 0, 0:TP], amask[:, :], ALU.add).then_inc(ml["arg"], 1)
                    TT(arg[:, TP:3 * P], R[:, 0, P:TP], amask[:, 0:P], ALU.add).then_inc(ml["arg"], 1)
                    TT(arg[0:TS, 3 * P:3 * P + TS], R[0:TS, 0, TP:T], amask_s[:, :], ALU.add).then_inc(ml["arg"], 1)
                if o == 4:
                    dve.wait_ge(ml["d"], 3 * (n + 1))
                    dve.wait_ge(ml["qk"], n + 1)
                    dve.wait_ge(ml["e"], 2 * (n + 1))
                    TT(pm[:, 0:3 * P], dx[:, 0:3 * P], R[:, 2, 0:3 * P], ALU.mult).then_inc(ml["p"], 1)
                    TT(pm[0:TS, 3 * P:3 * P + TS], dx[0:TS, 3 * P:3 * P + TS], R[0:TS, 2, 3 * P:3 * P + TS], ALU.mult).then_inc(ml["p"], 1)
                    TT(qi[:, :], mW[:, j, TP:T], es[:, 0:TS], ALU.mult).then_inc(ml["q"], 1)
                    dve.wait_ge(ml["q"], 2 * n + 1)
                    TT(seq(qn[:, :], LS), seq(qi[:, :], LS), n0v[:, :, bass.ds(h, 1)].to_broadcast([P, NS, LS]), ALU.mult).then_inc(ml["q"], 1)
                if o == 7:
                    dve.wait_ge(ml["dn"], n + 1)
                    dve.wait_ge(ml["out"], 2 * n + FREE)
                    TT(dn[:, :], dn[:, :], em[:, :], ALU.max).then_inc(ml["h"], 1)
                    dve.wait_ge(ml["h"], 4 * n + 1)
                    nc.vector.reciprocal(dn[:, :], dn[:, :]).then_inc(ml["h"], 1)
                    dve.wait_ge(ml["h"], 4 * n + 2)
                    for v in range(2):
                        TT(hh[:, v, :], R[:, 1 + v, 0:T], dn[:, :], ALU.mult).then_inc(ml["h"], 1)
                if o == 9:
                    dve.wait_ge(ml["r"], 2 * (n + 1))
                    for v in range(2):
                        STT(hh[:, v, :], hh[:, v, :], mlw[:, v, bass.ds(h, 1)], dn[:, :], ALU.mult, ALU.mult).then_inc(ml["y"], 1)
                    dve.wait_ge(ml["st1"], n + 1)
                    dve.wait_ge(ml["cs"], 2 * (n + 1))
                    dve.wait_ge(ml["stored"], n + FREE)
                    TT(C0[:, 0:4, :].rearrange("p a b -> p (a b)"), C0[:, 0:4, :].rearrange("p a b -> p (a b)"), Rf[:, 1024:2048], ALU.add).then_inc(ml["c"], 1)
                    nc.vector.tensor_copy(Cp[:, :], R[:, 1, 0:MV]).then_inc(ml["c"], 1)
                    nc.vector.tensor_copy(nnew[:, 0, bass.ds(h, 1)], R[:, 1, MV:MV + 1]).then_inc(ml["c"], 1)
                    TT(nnew[:, 1:NB, bass.ds(h, 1)], ndec[:, :].rearrange("p (b a) -> p b a", a=1), R[:, 1, MV + 1:MV + 1 + NS].rearrange("p (b a) -> p b a", a=1), ALU.add).then_inc(ml["c"], 1)
                if o == 11:
                    dve.wait_ge(ml["st2"], n + 1)
                    TT(C0[:, 4:8, :].rearrange("p a b -> p (a b)"), C0[:, 4:8, :].rearrange("p a b -> p (a b)"), Rf[:, 1024:2048], ALU.add).then_inc(ml["c2"], 1)

            n0v = par[:, 3, 44:108].rearrange("p (b h) -> p b h", h=MH)
            mlw = par[:, 1, 16:32].rearrange("p (h v) -> p v h", v=2)

            for k in range(HG_STEP):
                lo(S_HG, k + LEAD)
            dve.wait_ge(hg["zero"], 3)
            with dve.Fori(0, 3) as i:
                for k in range(HG_STEP):
                    lo(S_HG + HG_STEP + HG_STEP * i, k + LEAD)
                    for j, o in HG_AT[k]:
                        hg_step(j, o, 4 * i + j, i)
            for k in range(ML_STEP):
                lo(S_ML, k + LEAD)
                for j, o in HG_AT_ML[k]:
                    hg_step(j, o, 12 + j, 3)
            dve.wait_ge(hg["out"], HH + FREE)
            dve.wait_ge(hg["st"], 32 * HH)
            with dve.Fori(0, 3) as i:
                for k in range(ML_STEP):
                    lo(S_ML + ML_STEP + ML_STEP * i, k + LEAD)
                    for j, o in ML_AT[k]:
                        ml_step(j, o, 2 * i + j, i)
            for p in range(4):
                for k in range(8):
                    lo(S_ADA2 + 8 * p, k + LEAD)
                    if k % 4 == 3:
                        b = k // 4
                        mt = 32 + 4 * p + 2 * b
                        dve.wait_ge(used, S_ADA2 + 8 * p + k + 1 + FREE)
                        TT(mod[:, mt:mt + 2, :], ps[:, b, :, 0:NB], rep_last(bias_row[:, mt:mt + 2], NB), ALU.add).then_inc(bank_free[b], 1)
                    for j, o in ML_AT[8 * p + k]:
                        ml_step(j, o, 6 + j, 3)
            for g in range(4):
                dve.wait_ge(xhi, 4 + g + 1)
                TT(xl[:, 4 * g:4 * g + 4, :], merged[:, 4 * g:4 * g + 4, :], xh[:, 4 * g:4 * g + 4, :].bitcast(F32), ALU.subtract).then_inc(xlo, 1)
            with dve.Fori(0, 12) as i:
                ada(S_ADA2 + 32 + 8 * i, Q_ADA2 + 4 + i, 48 + 4 * i)
            dve.wait_ge(back_x, 16)
            with dve.Fori(0, 4) as i:
                C = S_OUT + 8 * i
                for k in range(8):
                    lo(C, k + LEAD)
                    if k % 4 == 3:
                        b = k // 4
                        kt = bass.ds(4 * i + 2 * b, 2)
                        g1 = mod[:, bass.ds(2 * KT + 4 * i + 2 * b, 2), :]
                        dve.wait_ge(used, C + k + 1 + FREE)
                        TT(mixo[:, kt, 0:TP], ps[:, b, :, 0:TP], g1[:, :, 0:1].to_broadcast([P, 2, TP]), ALU.mult).then_inc(x1_m, 1)
                        TT(seq3(mixo[:, kt, TP:T], LS), seq3(ps[:, b, :, TP:T], LS), rep3(g1[:, :, 1:NB], LS), ALU.mult).then_inc(bank_free[b], 1)
                        dve.wait_ge(bank_free[b], Q_OUT + i + 1 + FREE)
                        TT(xT2[:, kt, :], xT2[:, kt, :], mixo[:, kt, :], ALU.add).then_inc(x1_a, 1)
            modulate(2, xT2, mixo, 3 * KT, 4 * KT)
            dve.wait_ge(zab, 2)
            dve.wait_ge(spill_1, 16)
            cb = par[:, 1, 48:92]
            cw = [par[:, 2, 0:44], par[:, 2, 44:88], par[:, 3, 0:44]]
            with dve.Fori(0, 22) as i:
                C = S_UP + 8 * i
                for k in range(8):
                    lo(C, k + LEAD)
                    if k == 4:
                        dve.wait_ge(bank_free[0], Q_UP + i + 1 + FREE)
                        dve.wait_ge(ab_lead, i + 1)
                        for m in range(2):
                            c1 = bass.ds(2 * i + m, 1)
                            TSC(acv[:, m, 0:AB - 2], abuf[:, m, 0:AB - 2], cw[0][:, c1], cb[:, c1], ALU.mult, ALU.add).then_inc(ff_conv, 1)
                        for w in (1, 2):
                            for m in range(2):
                                c1 = bass.ds(2 * i + m, 1)
                                dve.wait_ge(ff_conv, 6 * i + 2 * (w - 1) + m + 1 + FREE)
                                STT(acv[:, m, 0:AB - 2], abuf[:, m, w:w + AB - 2], cw[w][:, c1], acv[:, m, 0:AB - 2], ALU.mult, ALU.add).then_inc(ff_conv, 1)
                    if k == 7:
                        dve.wait_ge(used, C + 8 + FREE)
                        dve.wait_ge(ff_gelu, i + 1)
                        dve.wait_ge(ff_lo, i + FREE)
                        TT(yb[:, :, 0:TP], acv[:, :, 0:TP], ps[:, 1, :, 0:TP], ALU.mult).then_inc(ff_y, 1)
                        for m in range(2):
                            x = TT(seq(yb[:, m, TP:T], LS), seq(acv[:, m, 2 + TP:AB], 2 + LS)[:, :, 0:LS], seq(ps[:, 1, m, TP:T], LS), ALU.mult)
                            x.then_inc((ff_y, bank_free[1])[m], 1)
                        dve.wait_ge(ff_hi, i + 1)
                        TT(ffl[:, bass.ds(2 * i, 2), :], yb[:, :, :], ffh[:, bass.ds(2 * i, 2), :].bitcast(F32), ALU.subtract).then_inc(ff_lo, 1)

            def down(i):
                for k in range(44):
                    if not isinstance(i, int) or S_DOWN + 44 * i + k + LEAD < S_END:
                        lo(S_DOWN + 44 * i, k + LEAD)
                    if k % 11 == 10:
                        b = 4 * i + k // 11
                        kt = slice(2 * b, 2 * b + 2)
                        g2 = mod[:, 5 * KT + 2 * b:5 * KT + 2 * b + 2, :]
                        if b == 0:
                            dve.wait_ge(back_1, 16)
                        dve.wait_ge(used, S_DOWN + 44 * i + k + 1 + FREE)
                        TT(dno[:, kt, 0:TP], ps[:, b % 2, :, 0:TP], g2[:, :, 0:1].to_broadcast([P, 2, TP]), ALU.mult).then_inc(x2_m, 1)
                        TT(seq3(dno[:, kt, TP:T], LS), seq3(ps[:, b % 2, :, TP:T], LS), rep3(g2[:, :, 1:NB], LS), ALU.mult).then_inc(bank_free[b % 2], 1)
                        dve.wait_ge(bank_free[b % 2], Q_DOWN + b // 2 + 1 + FREE)
                        TT(x1f[:, kt, :], x1f[:, kt, :], dno[:, kt, :], ALU.add).then_inc(x2_a, 1)
            down(0)
            down(1)
            dve.wait_ge(rs_done, 6)
            for kt in range(KT):
                STT(yT[:, kt, :], x1f[:, kt, :], par[:, 1, 32 + kt:33 + kt], rstd[:, :], ALU.mult, ALU.mult).then_inc(y_w, 1)
            for e in range(1, 12, 2):
                dve.wait_ge(y_t, e + 1)
                dve.wait_ge(y_c, e)
                w = P if e < 8 else TS
                nc.vector.tensor_copy(ytm[0:w, e // 4, 512 * (e % 4):512 * (e % 4) + 512], R[0:w, 1 + e % 3, :]).then_inc(y_c, 1)

        @block.gpsimd
        def _(pool):
            G, SEL = nc.gpsimd.tensor_tensor, nc.gpsimd.affine_select
            for s in (hg["out"], hg["stored"], ml["out"], ml["stored"], x1_acc, ab_tail):
                pool.sem_inc(s, FREE)
            cnt = [0]

            def cst_(ins):
                cnt[0] += 1
                ins.then_inc(const, 1)
                pool.wait_ge(const, cnt[0])
            cst_(nc.gpsimd.memset(ident[:, :], 0.0))
            cst_(SEL(out=ident[:, :], in_=ident[:, :], compare_op=ALU.not_equal, fill=1.0, base=0, pattern=[[-1, P]], channel_multiplier=1))
            cst_(nc.gpsimd.memset(ones[:, :], 1.0))
            cst_(nc.gpsimd.memset(ones8[:, :], 1.0))
            cst_(nc.gpsimd.memset(epsc[:, :], EPS))
            cst_(nc.gpsimd.memset(onec[:, :], 1.0))
            cst_(nc.gpsimd.memset(reset[:, :], 1.0))
            cst_(nc.gpsimd.memset(seq(reset[:, 0:TP], SUB)[:, :, 0:1], 0.0))
            cst_(nc.gpsimd.memset(seq(reset[:, TP:T], LS)[:, :, 0:1], 0.0))
            cst_(nc.gpsimd.memset(reset8[:, 0, :], 1.0))
            cst_(nc.gpsimd.memset(seq(reset8[:, 0, TP:T], LS)[:, :, 0:1], 0.0))
            cst_(nc.gpsimd.memset(reset8[:, 1, :], 0.0))
            cst_(nc.gpsimd.memset(reset8[:, 1, 0:1], NEG))
            cst_(nc.gpsimd.memset(seq(reset8[:, 1, TP:T], LS)[:, :, 0:1], NEG))
            for m, im, n, sub in ((maskf, hmask, P, SUB), (maskf_s, hmask_s, TS, LS)):
                cst_(nc.gpsimd.memset(m[:, :], 1.0))
                cst_(SEL(out=m[:, :], in_=m[:, :], compare_op=ALU.is_ge, fill=0.0, base=0, pattern=[[1, n]], channel_multiplier=-1))
                cst_(SEL(out=seq(m[:, :], sub), in_=seq(m[:, :], sub), compare_op=ALU.is_ge, fill=0.0, base=0, pattern=[[-sub, n // sub], [0, sub]], channel_multiplier=1))
                cst_(nc.gpsimd.tensor_copy(im[:, :], m[:, :]))
            cst_(nc.gpsimd.memset(amask[:, :], 0.0))
            cst_(SEL(out=amask[:, :], in_=amask[:, :], compare_op=ALU.is_ge, fill=NEG, base=0, pattern=[[1, TP]], channel_multiplier=-1))
            cst_(nc.gpsimd.tensor_scalar(amask_s[:, :], maskf_s[:, :], -NEG, NEG, ALU.mult, ALU.add))
            cst_(nc.gpsimd.memset(bmask[:, :], 1.0))
            cst_(SEL(out=bmask[:, :], in_=bmask[:, :], compare_op=ALU.is_ge, fill=0.0, base=0, pattern=[[-LS, NS]], channel_multiplier=1))
            cst_(SEL(out=bmask[:, :], in_=bmask[:, :], compare_op=ALU.is_ge, fill=0.0, base=LS - 1, pattern=[[LS, NS]], channel_multiplier=-1))
            assert cnt[0] == CONST_ALL
            pool.wait_ge(x_c, KT)
            pool.dma_start(xT_spill, xT[:].rearrange("p a b -> p (a b)")).then_inc(spill_x, 16)
            pool.wait_ge(row_d, ROW_WK)
            with nc.allow_non_contiguous_dma(reason="72 values"):
                pool.dma_start(m_p[0].rearrange("b h -> h b"), merged[0:MH, 11, 0:1]).then_inc(st_m, 16)
                pool.dma_start(m_s[0].rearrange("b h -> h b"), merged[0:MH, 11, 1:NB]).then_inc(st_m, 16)
            pool.wait_ge(xlo, 4)
            pool.wait_ge(spill_x, 16)
            pool.wait_ge(st_m, 32)
            pool.wait_ge(cv_c, 2)
            pool.wait_ge(gmm, 1)
            pool.wait_ge(row_t, 1)
            nc.gpsimd.memset(PT[:, :, :], 0.0).then_inc(hg["zero"], 1)
            nc.gpsimd.memset(PTs[:, :], 0.0).then_inc(hg["zero"], 1)
            nc.gpsimd.memset(Vx[:, :, :, :], 0.0).then_inc(hg["zero"], 1)
            pool.wait_ge(hg["zero"], 3)

            def hg_prologue(i):
                pool.wait_ge(hg["sig"], 4 * (i + 1))
                pool.wait_ge(hg["out"], 4 * i + FREE)
                G(W[:, 0], W[:, 0], S[:, 0], ALU.mult).then_inc(hg["pre"], 1)
                nc.gpsimd.tensor_copy(W[:, 2], S[:, 2]).then_inc(hg["pre"], 1)
                G(W[:, 3], W[:, 3], S[:, 3], ALU.mult).then_inc(hg["pre"], 1)
                pool.wait_ge(hg["pre"], 4 * i + 3)
                G(W[:, 3], W[:, 3], W[:, 4], ALU.mult).then_inc(hg["pre"], 1)

            def hg_step(j, o, n, i):
                h = n
                if o == 0:
                    pool.dma_start(S0[:, :, :], state_hgrn[0].rearrange("b h k v -> h k b v")[bass.ds(h, 1)].rearrange("o k b v -> (o k) b v")).then_inc(hg["s0"], 16)
                if o == 1:
                    pool.wait_ge(hg["qk"], 2 * (n + 1))
                    G(seq(kh[:, 0:TP], SUB), seq(kt_[:, 0:TP], SUB), seq(e1[:, 0:TP], SUB)[:, :, SUB - 1:SUB].to_broadcast([P, NSUB, SUB]), ALU.mult).then_inc(hg["dk"], 1)
                    G(seq(kh[:, TP:T], LS), seq(kt_[:, TP:T], LS), seq(e1[:, TP:T], LS)[:, :, LS - 1:LS].to_broadcast([P, NS, LS]), ALU.mult).then_inc(hg["dk"], 1)
                    G(seq(qs[:, :], SUB), seq(qt[:, 0:TP], SUB), rep_last(er[:, :], SUB), ALU.mult).then_inc(hg["dk"], 1)
                    G(dec[:, :], er[:, :], seq(e1[:, 0:TP], SUB)[:, :, SUB - 1], ALU.mult).then_inc(hg["dk"], 1)
                if o == 3:
                    count = known(pool, 4 * (n + 1))
                    pool.wait_ge(const, CONST_ALL)
                    pool.wait_ge(hg["tok"], count)
                    G(Vxs[:, :, :], mid(Vts[:, :], NS), rep_last(bmask[:, :], P), ALU.mult).then_inc(hg["vx"], 1)
                    for u in range(4):
                        rows_ = slice(SUB * u, SUB * (u + 1))
                        nc.gpsimd.tensor_copy(Vx[rows_, :, u, :], Vt[rows_, :, :]).then_inc(hg["vx"], 1)
                if o == 6:
                    pool.wait_ge(hg["o"], n + 1)
                    G(S0[:, :, :], S0[:, :, :], seq(e1[:, TP:T], LS)[:, :, LS - 1:LS].to_broadcast([P, NS, P]), ALU.mult).then_inc(hg["scaled"], 1)
                if o == 9:
                    pool.wait_ge(hg["y"], n + 1 + FREE)
                    G(merged[:, bass.ds(h, 1), :].rearrange("p a b -> p (a b)"), e1[:, :], W[:, 3, j, :], ALU.mult).then_inc(hg["out"], 1)
                    count = known(pool, n + 1 + FREE)
                    pool.wait_ge(const, CONST_ALL)
                    pool.wait_ge(hg["snew"], count)
                    pool.dma_start(hg_s[0].rearrange("b h k v -> h k b v")[bass.ds(h, 1)].rearrange("o k b v -> (o k) b v"), S0[:, :, :]).then_inc(hg["st"], 16)
                    pool.dma_start(hg_p[0, 0, bass.ds(h, 1)].rearrange("o k v -> (o k) v"), Sst[:, NSUB - 1, :]).then_inc(hg["st"], 16)
                    pool.wait_ge(hg["st"], 32 * (n + 1))
                    pool.sem_inc(hg["stored"], 1)

            def ml_prologue(i):
                count = known(pool, 4 * (i + 1))
                pool.wait_ge(const, CONST_ALL)
                pool.wait_ge(ml["sig"], count)
                pool.wait_ge(ml["out"], 4 * i + FREE)
                G(mW[:, 8:12, :], mW[:, 8:12, :], mS[:, 12:16, :], ALU.mult).then_inc(ml["pre"], 1)
                nc.gpsimd.tensor_copy(mW[:, 4:8, :], mS[:, 4:8, :]).then_inc(ml["pre"], 1)

            def ml_step(j, o, n, i):
                h = n
                if o == 0:
                    pool.dma_start(C0[:, :, :], state_mlstm_C[0].rearrange("b h k v -> h k b v")[bass.ds(h, 1)].rearrange("o k b v -> (o k) b v")).then_inc(ml["c0"], 16)
                if o == 5:
                    pool.wait_ge(ml["v"], 2 * (n + 1))
                    G(mVx[:, :, :], mid(mV[0:TS, 2, :], NS), rep_last(bmask[:, :], MV), ALU.mult).then_inc(ml["vx"], 1)
                if o == 7:
                    pool.wait_ge(ml["num"], n + 1)
                    G(C0[:, :, :], C0[:, :, :], rep_last(es[:, TS:TS + NS], MV), ALU.mult).then_inc(ml["cs"], 1)
                    G(ndec[:, :].rearrange("p (b a) -> p b a", a=1), es[:, TS:TS + NS].rearrange("p (b a) -> p b a", a=1), n0v[:, :, bass.ds(h, 1)], ALU.mult).then_inc(ml["cs"], 1)
                if o == 10:
                    pool.wait_ge(ml["y"], 2 * (n + 1))
                    G(hh[:, :, :], hh[:, :, :], mW[:, 8 + 2 * j:10 + 2 * j, :], ALU.mult).then_inc(ml["out"], 1)
                    pool.wait_ge(ml["out"], 2 * n + 1 + FREE)
                    mg = merged[:, bass.ds(2 * h, 2), :]
                    G(mg, mg, hh[:, :, :], ALU.add).then_inc(ml["out"], 1)
                if o == 11:
                    count = known(pool, n + 1 + FREE)
                    pool.wait_ge(const, CONST_ALL)
                    pool.wait_ge(ml["c2"], count)
                    pool.dma_start(C_s[0].rearrange("b h k v -> h k b v")[bass.ds(h, 1)].rearrange("o k b v -> (o k) b v"), C0[:, :, :]).then_inc(ml["st"], 16)
                    pool.dma_start(C_p[0, 0, bass.ds(h, 1)].rearrange("o k v -> (o k) v"), Cp[:, :]).then_inc(ml["st"], 16)
                    pool.wait_ge(ml["st"], 32 * (n + 1))
                    pool.sem_inc(ml["stored"], 1)

            n0v = par[:, 3, 44:108].rearrange("p (b h) -> p b h", h=MH)
            with pool.Fori(0, 3) as i:
                hg_prologue(i)
                for k in range(HG_STEP):
                    for j, o in HG_AT[k]:
                        hg_step(j, o, 4 * i + j, i)
            hg_prologue(3)
            for k in range(ML_STEP):
                for j, o in HG_AT_ML[k]:
                    hg_step(j, o, 12 + j, 3)
            pool.wait_ge(hg["st"], 32 * HH)
            with pool.Fori(0, 3) as i:
                ml_prologue(i)
                for k in range(ML_STEP):
                    for j, o in ML_AT[k]:
                        ml_step(j, o, 2 * i + j, i)
            ml_prologue(3)
            for k in range(ML_STEP):
                for j, o in ML_AT[k]:
                    ml_step(j, o, 6 + j, 3)
            pool.wait_ge(n_c, 1)
            pool.dma_start(n_p[0, 0], ntok[0:MH, :]).then_inc(st_n, 16)
            pool.dma_start(n_s[0].rearrange("b h d -> (b h) d"), ntok[MH:, :]).then_inc(st_n, 16)
            pool.wait_ge(ml["st"], 32 * MH)
            pool.dma_start(xT2[:].rearrange("p a b -> p (a b)"), xT_spill).then_inc(back_x, 16)
            nc.gpsimd.memset(sqacc[:, :, :], 0.0).then_inc(zab, 1)
            pool.wait_ge(zab, 1)
            with pool.Fori(0, 4) as i:
                pool.wait_ge(x1_sq, i + 1)
                pool.wait_ge(x1_acc, i + FREE)
                G(sqacc[:, :, :], sqacc[:, :, :], mixo[:, bass.ds(4 * i, 4), :], ALU.add).then_inc(x1_acc, 1)
            pool.wait_ge(x1_a, 8)
            pool.dma_start(x1_spill, xT2[:].rearrange("p a b -> p (a b)")).then_inc(spill_1, 16)
            pool.wait_ge(xlo, 12)
            pool.wait_ge(st_n, 32)
            nc.gpsimd.memset(abuf[:, :, 0:2], 0.0).then_inc(zab, 1)
            with pool.Fori(0, 22) as i:
                count = known(pool, 6 * i + FREE)
                pool.wait_ge(const, CONST_ALL)
                pool.wait_ge(ff_conv, count)
                leads = seq3(abuf[:, :, 2 + TP:AB], 2 + LS)
                pool.wait_ge(ab_tail, 2 * i + FREE)
                for m in range(2):
                    x = nc.gpsimd.tensor_copy(seq(abuf[:, m, 2 + TP:AB], 2 + LS)[:, :, 0:2], cst[:, bass.ds(2 * i + m, 1), :].rearrange("p o (b j) -> p (o b) j", j=2))
                x.then_inc(ab_lead, 1)
                count = known(pool, Q_UP + i + 1 + FREE)
                pool.wait_ge(const, CONST_ALL)
                pool.wait_ge(bank_free[0], count)
                nc.gpsimd.tensor_copy(tails[:, bass.ds(2 * i, 2), 0:2], abuf[:, :, TP:TP + 2]).then_inc(ab_tail, 1)
                for m in range(2):
                    x = nc.gpsimd.tensor_copy(tails[:, bass.ds(2 * i + m, 1), 2:].rearrange("p o (b j) -> p (o b) j", j=2), seq(abuf[:, m, 2 + TP:AB], 2 + LS)[:, :, LS:LS + 2])
                x.then_inc(ab_tail, 1)
            pool.wait_ge(used, S_DOWN + FREE)
            pool.dma_start(x1f[:].rearrange("p a b -> p (a b)"), x1_spill).then_inc(back_1, 16)
            pool.wait_ge(ff_lo, 22 + FREE)
            nc.gpsimd.memset(sqf[:, :, :], 0.0).then_inc(zab, 1)
            pool.wait_ge(zab, 3)
            for b in range(8):
                for g in range(11):
                    if b < 2 and g // 6 == b:
                        pool.wait_ge(tl_c, g + 1)
                        pool.dma_start(cv_p[0, 0, :, 512 * g:512 * g + 512], cts[0:2, g % 2, :]).then_inc(st_cv[g % 2], 16)
                        pool.dma_start(cv_s[0].rearrange("b j f -> (b j) f")[:, 512 * g:512 * g + 512], cts[2:2 + NS * 2, g % 2, :]).then_inc(st_cv[g % 2], 16)
                pool.wait_ge(x2_sq, b + 1)
                pool.wait_ge(x2_acc, b)
                G(sqf[:, :, :], sqf[:, :, :], sqd[:, :, :], ALU.add).then_inc(x2_acc, 1)


_INS = ['x_prompt', 'x_sample', 'c_prompt', 'c_sample', 'state_hgrn', 'state_mlstm_C', 'state_mlstm_n', 'state_mlstm_m',
        'state_conv', 'ada_w', 'ada_b', 'w_in', 'hg_lb_logits', 'hg_norm_w', 'ml_i_bias', 'ml_f_bias', 'ml_norm_w', 'w_out',
        'conv_w', 'conv_b', 'w_up', 'w_down', 'final_norm_w']
_OUTS = [(1, 256, 2048), (8, 4, 2048), (1, 1, 16, 128, 128), (1, 8, 16, 128, 128), (1, 1, 8, 128, 256), (1, 8, 8, 128, 256),
         (1, 1, 8, 128), (1, 8, 8, 128), (1, 1, 8), (1, 8, 8), (1, 1, 2, 5632), (1, 8, 2, 5632)]


def kernel(**inputs):
    import concourse.bacc as _bacc
    from concourse.bass_utils import run_bass_kernel_spmd as _run

    nc = _bacc.Bacc("TRN2", target_bir_lowering=False, num_devices=1)
    arrays, args = {}, []
    for name in _INS:
        a = np.ascontiguousarray(inputs[name])
        arrays[f"in_{name}"] = a
        args.append(nc.dram_tensor(f"in_{name}", a.shape, mybir.dt.from_np(a.dtype), kind="ExternalInput").ap())
    for i, shape in enumerate(_OUTS):
        args.append(nc.dram_tensor(f"out_{i}", shape, F32, kind="ExternalOutput").ap())
    build(nc, *args)
    r = _run(nc, [arrays], core_ids=[0])
    return tuple(r.results[0][f"out_{i}"] for i in range(len(_OUTS)))
```

```python
from contextlib import ExitStack

import numpy as np

import concourse.bass as bass
from concourse import mybir

F32 = mybir.dt.float32
F32R = mybir.dt.float32r
I32 = mybir.dt.int32
ALU = mybir.AluOpType
ACT = mybir.ActivationFunctionType

P = 128
D = 2048
KT = D // P
TP = 256
NS = 8
LS = 4
TS = NS * LS
T = TP + TS
NB = 1 + NS
EPS = 1e-6
HH = 16
MH = 8
MV = 256
FF = 5632
FT = FF // P
CW = 3
SUB = 32
NSUB = TP // SUB
HSC = float(P) ** -0.5
NEG = -1.0e30
ROW_WK = 16
ROW_T = ROW_WK
CONST_ALL = 31
X_FREE = 2
FREE = 1
LEAD = 3
RING = 4
KC = 4
CN = 256

C_HQ, C_HF, C_HI, C_HG = 0, 2048, 4096, 6144
C_MQ, C_MK, C_MV, C_MI, C_MF, C_MO = 8192, 9216, 10240, 12288, 12296, 12304
C_GA, C_GB = 14352, 16400

HG_BLOCKS = "ssassssassss"
ML_BLOCKS = "ssassassasas"
HG_STEP = 4 * len(HG_BLOCKS)
ML_STEP = 4 * len(ML_BLOCKS)
N_ADA1 = (0, 0)
N_HG = (64, 8)
N_ML = (N_HG[0] + 4 * HG_STEP, N_HG[1] + 4 * len(HG_BLOCKS) // 2)
N_ADA2 = (N_ML[0] + 4 * ML_STEP, N_ML[1] + 4 * len(ML_BLOCKS) // 2)
N_OUT = (N_ADA2[0] + 32, N_ADA2[1] + 4)
N_UP = (N_OUT[0] + 32, N_OUT[1] + 4)
N_DOWN = (N_UP[0] + 176, N_UP[1] + 22)


def ahead(base, i, chunks, pairs):
    return base[0] + i * chunks, base[1] + i * pairs


def hg_base(i):
    return ahead(N_HG, i, HG_STEP, len(HG_BLOCKS) // 2)


def ml_base(i):
    return ahead(N_ML, i, ML_STEP, len(ML_BLOCKS) // 2)


def ada1_base(i):
    return ahead(N_ADA1, i, 8, 1)


def ada2_base(i):
    return ahead(N_ADA2, i, 8, 1)


def out_base(i):
    return ahead(N_OUT, i, 8, 1)


def up_base(i):
    return ahead(N_UP, i, 8, 1)


def down_base(i):
    return ahead(N_DOWN, i, 44, 2)


A_HG = 16
A_ML = A_HG + 4 * HG_BLOCKS.count("a")
A_ADA2 = A_ML + 4 * ML_BLOCKS.count("a")


def ada_before(b, kinds):
    return kinds[:b].count("a")


HG_NSTEP = 10
ML_NSTEP = 12


def steps_at(k, first, chunks, nsteps, heads):
    return [(j, o) for j in range(heads) for o in range(nsteps)
            if first + (j * nsteps + o) * (chunks - first) // (heads * nsteps) == k]


def build(nc, x_prompt, x_sample, c_prompt, c_sample, state_hgrn, state_mlstm_C, state_mlstm_n, state_mlstm_m,
          state_conv, ada_w, ada_b, w_in, hg_lb_logits, hg_norm_w, ml_i_bias, ml_f_bias, ml_norm_w, w_out,
          conv_w, conv_b, w_up, w_down, final_norm_w,
          y_prompt, y_sample, hg_p, hg_s, C_p, C_s, n_p, n_s, m_p, m_s, cv_p, cv_s):
    xT_spill = nc.dram_tensor("xT_spill", (P, KT * T), F32).ap()
    x1_spill = nc.dram_tensor("x1_spill", (P, KT * T), F32).ap()
    with ExitStack() as ctx:
        def sb(name, shape, dt=F32, stack=ctx):
            return stack.enter_context(nc.sbuf_tensor(name, shape, dt))

        def sem(name):
            return ctx.enter_context(nc.semaphore(name))

        raw = sb("raw", [P, RING, KC, CN])
        whi = sb("whi", [P, RING, KC, CN], F32R)
        wlo = sb("wlo", [P, RING, KC, CN], F32R)
        split = ExitStack()
        xh = sb("xh", [P, KT, T], F32R, stack=split)
        xl = sb("xl", [P, KT, T], F32R, stack=split)
        split.close()
        dno = sb("dno", [P, KT, T])
        x1f = sb("x1f", [P, KT, T])
        mod = sb("mod", [P, 6 * KT, NB])
        par = sb("par", [P, 4, P])
        cst = sb("cst", [P, FT, NS * 2])
        ident = sb("ident", [P, P])
        ones = sb("ones", [P, P])
        epsc = sb("epsc", [P, 1])
        onec = sb("onec", [P, 1])
        rstd = sb("rstd", [P, T])
        lnms = sb("lnms", [P, T])

        setup = ExitStack()
        mixer = ExitStack()
        ffn = ExitStack()
        cT = sb("cT", [P, KT, NB], stack=mixer)
        cs = sb("cs", [P, KT, 2 * NB], F32R, stack=mixer)
        arows = sb("arows", [2 * NB, 2, CN], stack=mixer)
        sel = sb("sel", [2 * NB, NB], stack=mixer)
        merged = sb("merged", [P, KT, T], stack=mixer)
        lbc = sb("lbc", [P, 2, HH], stack=mixer)
        lbt = sb("lbt", [P, 2, HH], stack=mixer)
        hmask = sb("hmask", [P, P], I32, stack=mixer)
        hmask_s = sb("hmask_s", [TS, TS], I32, stack=mixer)
        maskf = sb("maskf", [P, P], stack=mixer)
        maskf_s = sb("maskf_s", [TS, TS], stack=mixer)
        reset = sb("reset", [P, T], stack=mixer)
        amask = sb("amask", [P, TP], stack=mixer)
        amask_s = sb("amask_s", [TS, TS], stack=mixer)
        bmask = sb("bmask", [TS, NS], stack=mixer)
        ones8 = sb("ones8", [MH, P], stack=mixer)
        acol = sb("acol", [P, 3, MH], stack=mixer)
        wkcol = sb("wkcol", [P, 3, MH], stack=mixer)
        LR = sb("LR", [MH, 2 * T + TS + NS], stack=mixer)
        nnew = sb("nnew", [P, NB, MH], stack=mixer)
        ntok = sb("ntok", [NB * MH, P], stack=mixer)
        LRW = 2 * T + TS + NS
        xT = sb("xT", [P, KT, T], stack=setup)
        xtm = sb("xtm", [P, 3, D], stack=setup)
        ctm = sb("ctm", [NB, D], stack=setup)
        cvr = sb("cvr", [NS * 2, FF], stack=setup)
        partm = sb("partm", [P, 4, P], stack=setup)
        gw = sb("gw", [P, KT, 2 * MH], stack=setup)
        gwh = sb("gwh", [P, KT, 2 * MH], F32R, stack=setup)
        gwl = sb("gwl", [P, KT, 2 * MH], F32R, stack=setup)
        gb = sb("gb", [MH, 2], stack=setup)
        m0 = sb("m0", [MH, NS], stack=setup)
        reset8 = sb("reset8", [MH, 2, T], stack=setup)
        setup.close()
        hg_mem = ExitStack()
        S = sb("S", [P, 5, 4, T], stack=hg_mem)
        W = sb("W", [P, 5, 4, T], stack=hg_mem)
        lf = sb("lf", [P, T], stack=hg_mem)
        bc = sb("bc", [P, T], stack=hg_mem)
        bm = sb("bm", [P, T], stack=hg_mem)
        e1 = sb("e1", [P, T], stack=hg_mem)
        e2 = sb("e2", [P, T], stack=hg_mem)
        er = sb("er", [P, NSUB], stack=hg_mem)
        dec = sb("dec", [P, NSUB], stack=hg_mem)
        qt = sb("qt", [P, T], stack=hg_mem)
        kt_ = sb("kt_", [P, T], stack=hg_mem)
        kh = sb("kh", [P, T], stack=hg_mem)
        qs = sb("qs", [P, TP], stack=hg_mem)
        PT = sb("PT", [P, 2, P], stack=hg_mem)
        PTs = sb("PTs", [TS, TS], stack=hg_mem)
        Vt = sb("Vt", [P, 2, P], stack=hg_mem)
        Vts = sb("Vts", [TS, P], stack=hg_mem)
        Kt = sb("Kt", [P, 2, P], stack=hg_mem)
        Kts = sb("Kts", [TS, P], stack=hg_mem)
        Vx = sb("Vx", [P, 2, 4, P], stack=hg_mem)
        Vxs = sb("Vxs", [TS, NS, P], stack=hg_mem)
        Sst = sb("Sst", [P, NSUB, P], stack=hg_mem)
        S0 = sb("S0", [P, NS, P], stack=hg_mem)
        hg_mem.close()
        ml_mem = ExitStack()
        mS = sb("mS", [P, 5 * 4, T], stack=ml_mem)
        mW = sb("mW", [P, 12, T], stack=ml_mem)
        mLR = sb("mLR", [MH, LRW], stack=ml_mem)
        em = sb("em", [P, T], stack=ml_mem)
        es = sb("es", [P, TS + NS], stack=ml_mem)
        arg = sb("arg", [P, 3 * P + TS], stack=ml_mem)
        dx = sb("dx", [P, 3 * P + TS], stack=ml_mem)
        pm = sb("pm", [P, 3 * P + TS], stack=ml_mem)
        qi = sb("qi", [P, TS], stack=ml_mem)
        qn = sb("qn", [P, TS], stack=ml_mem)
        mK = sb("mK", [P, 3, P], stack=ml_mem)
        mV = sb("mV", [P, 3, MV], stack=ml_mem)
        mVx = sb("mVx", [TS, NS, MV], stack=ml_mem)
        C0 = sb("C0", [P, NS, MV], stack=ml_mem)
        Cp = sb("Cp", [P, MV], stack=ml_mem)
        ndec = sb("ndec", [P, NS], stack=ml_mem)
        dn = sb("dn", [P, T], stack=ml_mem)
        hh = sb("hh", [P, 2, T], stack=ml_mem)
        hsq = sb("hsq", [P, 2, T], stack=ml_mem)
        ml_mem.close()
        post = ExitStack()
        mixo = sb("mixo", [P, KT, T], stack=post)
        xT2 = sb("xT2", [P, KT, T], stack=post)
        sqacc = sb("sqacc", [P, 4, T], stack=post)
        post.close()
        mixer.close()
        ffh = sb("ffh", [P, FT, T], F32R, stack=ffn)
        ffl = sb("ffl", [P, FT, T], F32R, stack=ffn)
        tails = sb("tails", [P, FT, 2 + NS * 2], stack=ffn)
        AB = 2 + TP + NS * (2 + LS)
        up = ExitStack()
        abuf = sb("abuf", [P, 2, AB], stack=up)
        acv = sb("acv", [P, 2, AB], stack=up)
        yb = sb("yb", [P, 2, T], stack=up)
        up.close()
        cts = sb("cts", [2 + NS * 2, 2, 512], stack=ffn)
        sqd = sb("sqd", [P, 2, T], stack=ffn)
        sqf = sb("sqf", [P, 2, T], stack=ffn)
        ffn.close()
        last = ExitStack()
        yT = sb("yT", [P, KT, T], stack=last)
        ytm = sb("ytm", [P, 3, D], stack=last)
        last.close()
        ps = ctx.enter_context(nc.psum_tensor("ps", [P, 2, 2, 512], F32))
        R = ctx.enter_context(nc.psum_tensor("R", [P, 4, 512], F32))
        Rf = R[:].rearrange("p a b -> p (a b)")

        landed = [sem(f"landed{i}") for i in range(RING)]
        hi_done = sem("hi_done")
        lo_done = sem("lo_done")
        used = sem("used")
        ada_rows = sem("ada_rows")
        ada_cols = sem("ada_cols")
        bank_free = [sem("bank_free0"), sem("bank_free1")]
        ld_c, ld_x, ld_par, ld_conv, ld_gw, ld_gs = (sem(n) for n in ("ld_c", "ld_x", "ld_par", "ld_conv", "ld_gw", "ld_gs"))
        const = sem("const")
        par_t, par_c = sem("par_t"), sem("par_c")
        c_silu, c_t, c_c, c_hi, c_lo = (sem(n) for n in ("c_silu", "c_t", "c_c", "c_hi", "c_lo"))
        cv_t, cv_c = sem("cv_t"), sem("cv_c")
        x_t, x_c, x_sum = sem("x_t"), sem("x_c"), sem("x_sum")
        sq_done, ms_done, rs_done, xn_done = (sem(n) for n in ("sq_done", "ms_done", "rs_done", "xn_done"))
        sc_one, md_p, md_s, xhi, xlo = (sem(n) for n in ("sc_one", "md_p", "md_s", "xhi", "xlo"))
        back_x, spill_1, back_1 = (sem(n) for n in ("back_x", "spill_1", "back_1"))
        lb_a, lb_d = sem("lb_a"), sem("lb_d")
        gw_hi, gw_lo, gmm, row_a, row_d, row_t, row_c = (sem(n) for n in ("gw_hi", "gw_lo", "gmm", "row_a", "row_d", "row_t", "row_c"))
        st_n, st_y, st_cv = sem("st_n"), sem("st_y"), [sem("st_cv0"), sem("st_cv1")]
        hg = {n: sem("hg_" + n) for n in ("zero", "sig", "pre", "logf", "b", "bm", "exp", "qk", "dk", "scores", "tr", "pt",
                                          "tok", "vx", "u", "state", "o", "us", "sq", "scaled", "snew", "ms", "rstd",
                                          "y", "out", "s0", "st")}
        ml = {n: sem("ml_" + n) for n in ("sig", "pre", "lr", "bc", "qk", "kT", "e", "k", "arg", "d", "p", "q", "vT", "v",
                                          "vx", "num", "dn", "h", "cs", "sq", "ms", "st1", "st2", "r", "y", "c", "c2",
                                          "out", "c0", "st")}
        n_t, n_c = sem("n_t"), sem("n_c")
        x1_m, x1_a, x1_sq, x1_acc = (sem(n) for n in ("x1_m", "x1_a", "x1_sq", "x1_acc"))
        ab_ready, ab_lead, ab_tail = sem("ab_ready"), sem("ab_lead"), sem("ab_tail")
        ff_conv, ff_gelu, ff_y, ff_hi, ff_lo = (sem(n) for n in ("ff_conv", "ff_gelu", "ff_y", "ff_hi", "ff_lo"))
        tl_t, tl_c = sem("tl_t"), sem("tl_c")
        x2_m, x2_a, x2_sq, x2_acc = (sem(n) for n in ("x2_m", "x2_a", "x2_sq", "x2_acc"))
        y_w, y_t, y_c = sem("y_w"), sem("y_t"), sem("y_c")
        zab = sem("zab")

        ada_v = ada_w[0].rearrange("(kt p) n -> p kt n", p=P)
        win_v = w_in[0].rearrange("(kt p) n -> p kt n", p=P)
        out_v = w_out[0].rearrange("(kt p) n -> p kt n", p=P)
        up_v = w_up[0].rearrange("(kt p) n -> p kt n", p=P)
        down_v = w_down[0].rearrange("(kt p) n -> p kt n", p=P)

        def known(eng, x):
            if not isinstance(x, int):
                eng.compute_val(x)
            return x

        def mid(a, n):
            return a.rearrange("p (a m) -> p a m", a=1).to_broadcast([a.shape[0], n, a.shape[1]])

        def rep_last(a, n):
            return a.rearrange("p (m a) -> p m a", a=1).to_broadcast([a.shape[0], a.shape[1], n])

        def rep3(a, n):
            return a.rearrange("p k (m a) -> p k m a", a=1).to_broadcast([a.shape[0], a.shape[1], a.shape[2], n])

        def seq(a, n):
            return a.rearrange("p (c t) -> p c t", t=n)

        def seq3(a, n):
            return a.rearrange("p k (c t) -> p k c t", t=n)

        def hg_cols(i):
            return [c + 512 * i + 256 * u for c in (C_HQ, C_HF, C_HI, C_HG, C_GA) for u in range(2)]

        def ml_cols(i):
            return [C_MQ + 256 * i, C_MK + 256 * i] + [c + 512 * i + 256 * u for c in (C_MV, C_MO, C_GB) for u in range(2)]

        HG_AT = [steps_at(k, 3, HG_STEP, HG_NSTEP, 4) for k in range(HG_STEP)]
        HG_AT_ML = [steps_at(k, 2, ML_STEP, HG_NSTEP, 4) for k in range(ML_STEP)]
        ML_AT = [steps_at(k, 1, ML_STEP, ML_NSTEP, 2) for k in range(ML_STEP)]
        ML_AT_ADA = [steps_at(k, 2, 32, ML_NSTEP, 2) for k in range(32)]
        bias_row = par[:, 0, :]

        block = ctx.enter_context(nc.Block())

        @block.sync
        def _(sp):
            def block256(N, b, view, col, chunks=4, first=False):
                for s in range(chunks):
                    k = chunks * b + s
                    if not first or k >= RING:
                        sp.wait_ge(lo_done, N[0] + k - 3)
                    sp.dma_start(raw[:, k % RING], view[:, KC * s:KC * (s + 1), bass.ds(col, CN)]).then_inc(landed[k % RING], 16)

            def pair(N, view, col, first=False):
                for u in range(2):
                    block256(N, u, view, col + CN * u, first=first)

            def hg_stream(i):
                for b, kind in enumerate(HG_BLOCKS):
                    a = ada_before(b, HG_BLOCKS)
                    if kind == "s":
                        block256(hg_base(i), b, win_v, hg_cols(i)[b - a])
                    else:
                        block256(hg_base(i), b, ada_v, CN * (A_HG + 2 * i + a))

            def ml_stream(i):
                for b, kind in enumerate(ML_BLOCKS):
                    a = ada_before(b, ML_BLOCKS)
                    if kind == "s":
                        block256(ml_base(i), b, win_v, ml_cols(i)[b - a])
                    else:
                        block256(ml_base(i), b, ada_v, CN * (A_ML + 4 * i + a))

            pair(ada1_base(0), ada_v, 0, first=True)
            with sp.Fori(1, 8) as i:
                pair(ada1_base(i), ada_v, 512 * i)
            with sp.Fori(0, 4) as i:
                hg_stream(i)
            with sp.Fori(0, 4) as i:
                ml_stream(i)
            with sp.Fori(0, 4) as i:
                pair(ada2_base(i), ada_v, CN * A_ADA2 + 512 * i)
            with sp.Fori(0, 4) as i:
                pair(out_base(i), out_v, 512 * i)
            with sp.Fori(0, 22) as i:
                for u in range(2):
                    block256(up_base(i), u, up_v, FF * u + CN * i)
            with sp.Fori(0, 2) as i:
                for u in range(4):
                    block256(down_base(i), u, down_v, 1024 * i + CN * u, chunks=11)
            for tt in range(3):
                sp.wait_ge(y_c, 4 * (tt + 1))
                if tt < 2:
                    sp.dma_start(y_prompt[0, P * tt:P * (tt + 1), :], ytm[:, tt, :]).then_inc(st_y, 16)
                else:
                    sp.dma_start(y_sample.rearrange("b t d -> (b t) d"), ytm[0:TS, 2, :]).then_inc(st_y, 16)
            sp.wait_ge(st_y, 48)
            sp.wait_ge(st_n, 32)
            sp.wait_ge(st_cv[0], 32 * 6)
            sp.wait_ge(st_cv[1], 32 * 5)
            sp.wait_ge(hg["st"], 32 * (HH + 1))
            sp.wait_ge(ml["st"], 32 * (MH + 1))
            sp.wait_ge(spill_1, 16)

        @block.tensor
        def _(pe):
            mm = nc.tensor.matmul

            def tr(out, in_):
                return nc.tensor.transpose(out, in_, ident[0:in_.shape[0], 0:in_.shape[0]])

            def chunk(c, k, first, last, bank, hi, lo, kt0):
                pe.wait_ge(lo_done, c + 1)
                s = k % RING
                for kk in range(KC):
                    for m in range(2):
                        cols = slice(P * m, P * (m + 1))
                        o = ps[:, bank, m, 0:T]
                        mm(o, whi[:, s, kk, cols], hi[:, kt0 + kk, :], start=first and kk == 0, stop=False)
                        mm(o, whi[:, s, kk, cols], lo[:, kt0 + kk, :], start=False, stop=False)
                        x = mm(o, wlo[:, s, kk, cols], hi[:, kt0 + kk, :], start=False, stop=last and kk == KC - 1)
                x.then_inc(used, 1)

            def ada_chunk(c, k, first, last, bank, kt0):
                pe.wait_ge(lo_done, c + 1)
                s = k % RING
                for kk in range(KC):
                    for w in (whi, wlo):
                        x = mm(ps[0:2 * NB, bank, 0, 0:CN], cs[:, kt0 + kk, :], w[:, s, kk, :], start=first and kk == 0 and w is whi,
                               stop=last and kk == KC - 1 and w is wlo)
                x.then_inc(used, 1)

            def ada_turn(n, bank):
                pe.wait_ge(ada_rows, n + 1)
                for m in range(2):
                    x = mm(ps[:, bank, 1, NB * m:NB * (m + 1)], arows[:, bank, P * m:P * (m + 1)], sel[:, :], start=True, stop=True)
                x.then_inc(ada_cols, 1)

            def stream(N, kinds, A0, hook=None, xparts=None):
                for b, kind in enumerate(kinds):
                    pe.wait_ge(bank_free[b % 2], N[1] + b // 2 + FREE)
                    for s in range(4):
                        k = 4 * b + s
                        if xparts is not None and b == 0:
                            pe.wait_ge(xlo, xparts + s + 1)
                        if kind == "s":
                            chunk(N[0] + k, k, s == 0, s == 3, b % 2, xh, xl, KC * s)
                        else:
                            ada_chunk(N[0] + k, k, s == 0, s == 3, b % 2, KC * s)
                        if s == 1 and b and kinds[b - 1] == "a":
                            ada_turn(A0 + ada_before(b - 1, kinds), (b - 1) % 2)
                        if hook is not None:
                            hook(k)
                if kinds[-1] == "a":
                    ada_turn(A0 + ada_before(len(kinds) - 1, kinds), (len(kinds) - 1) % 2)

            pe.sem_inc(used, FREE)
            pe.sem_inc(ml["bc"], FREE)
            pe.wait_ge(const, 4)
            pe.wait_ge(ld_c, 32)
            pe.wait_ge(c_silu, 1)
            for kt in range(KT):
                x = tr(R[:, 3, NB * kt:NB * (kt + 1)], ctm[0:NB, P * kt:P * (kt + 1)])
            x.then_inc(c_t, 1)
            pe.wait_ge(ld_par, 16 * 9)
            for t, r in enumerate((128, 92, 88, 108)):
                x = tr(R[:, 2, P * t:P * t + r], partm[0:r, t, :])
            x.then_inc(par_t, 1)
            pe.wait_ge(const, 9)
            pe.wait_ge(c_hi, 1)
            pe.wait_ge(c_lo, 1)
            pe.wait_ge(ld_x, 48)
            for i in range(4):
                def hook(k, i=i):
                    if k % 2:
                        kt = 4 * i + k // 2
                        pe.wait_ge(x_c, kt + X_FREE - 1)
                        for tt in range(3):
                            w = P if tt < 2 else TS
                            x = tr(R[:, k // 2 % 2, P * tt:P * tt + w], xtm[0:w, tt, P * kt:P * (kt + 1)])
                        x.then_inc(x_t, 1)
                stream(ada1_base(i), "aa", 2 * i, hook)
            pe.wait_ge(ld_conv, 16)
            for g in range(2):
                if g == 0:
                    pe.wait_ge(par_c, 1)
                    pe.wait_ge(c_c, 1)
                for ft in range(22 * g, 22 * g + 22):
                    x = tr(R[:, 2 + g, 16 * (ft - 22 * g):16 * (ft - 22 * g) + 16], cvr[:, P * ft:P * (ft + 1)])
                x.then_inc(cv_t, 1)
            pe.wait_ge(x_c, KT + X_FREE)
            pe.wait_ge(x_sum, KT)
            mm(R[:, 0, 0:T], ones[:, :], lnms[:, :], start=True, stop=True).then_inc(ms_done, 1)
            with pe.Fori(4, 8) as i:
                stream(ada1_base(i), "aa", 2 * i)
            pe.wait_ge(gw_lo, 1)
            pe.wait_ge(rs_done, 2)
            for g in range(2):
                for kt in range(KT):
                    pe.wait_ge(xlo, kt // KC + 1)
                    cols = slice(MH * g, MH * (g + 1))
                    o = R[0:MH, g, 0:T]
                    mm(o, gwh[:, kt, cols], xh[:, kt, :], start=kt == 0, stop=False)
                    mm(o, gwh[:, kt, cols], xl[:, kt, :], start=False, stop=False)
                    x = mm(o, gwl[:, kt, cols], xh[:, kt, :], start=False, stop=kt == KT - 1)
            x.then_inc(gmm, 1)

            def hg_step(j, o, n, i):
                if o == 2:
                    pe.wait_ge(hg["qk"], 2 * (n + 1))
                    pe.wait_ge(hg["snew"], n + FREE)
                    for t in range(2):
                        x = mm(R[:, 0, P * t:P * (t + 1)], kt_[:, P * t:P * (t + 1)], qt[:, P * t:P * (t + 1)], start=True, stop=True)
                    x = mm(R[0:TS, 0, TP:T], kt_[:, TP:T], qt[:, TP:T], start=True, stop=True)
                    x.then_inc(hg["scores"], 1)
                    pe.wait_ge(hg["pre"], 2 * (i + 1))
                    for dst, src, s in ((1, W[:, 2, j, :], 0), (2, kh, 1)):
                        if s:
                            pe.wait_ge(hg["dk"], 4 * (n + 1))
                            pe.wait_ge(hg["y"], n + FREE)
                        for t in range(2):
                            tr(R[:, dst, P * t:P * (t + 1)], src[:, P * t:P * (t + 1)])
                        tr(R[0:TS, dst, TP:TP + P], src[:, TP:T]).then_inc(hg["tr"], 1)
                if o == 4:
                    pe.wait_ge(hg["vx"], 5 * n + 4)
                    pe.wait_ge(hg["rstd"], 2 * n + FREE)
                    for t, bank in ((0, 3), (1, 1)):
                        mm(R[:, bank, :], Kt[:, t, :], Vx[:, t].rearrange("p a b -> p (a b)"), start=True, stop=True).then_inc(hg["u"], 1)
                if o == 6:
                    pe.wait_ge(hg["pt"], 2 * (n + 1))
                    pe.wait_ge(hg["state"], 8 * (n + 1))
                    pe.wait_ge(hg["s0"], 16 * (n + 1))
                    for t in range(2):
                        mm(R[:, 2, P * t:P * (t + 1)], Vt[:, t, :], PT[:, t, :], start=t == 0, stop=False, skip_group_check=True)
                    for c in range(1, NSUB):
                        mm(R[:, 2, SUB * c:SUB * (c + 1)], Sst[:, c - 1, :], qs[:, SUB * c:SUB * (c + 1)], start=False, stop=False, skip_group_check=True)
                    mm(R[:, 2, TP:T], Vts[:, :], PTs[:, :], start=False, stop=False, skip_group_check=True)
                    for b in range(NS):
                        x = mm(R[:, 2, TP + LS * b:TP + LS * (b + 1)], S0[:, b, :], qt[:, TP + LS * b:TP + LS * (b + 1)], start=False, stop=b == NS - 1, skip_group_check=True)
                    x.then_inc(hg["o"], 1)
                    pe.wait_ge(hg["vx"], 5 * (n + 1))
                    for u in range(2):
                        x = mm(R[:, u, :], Kts[:, :], Vxs[:, 4 * u:4 * u + 4, :].rearrange("p a b -> p (a b)"), start=True, stop=True)
                    x.then_inc(hg["us"], 1)
                if o == 8:
                    pe.wait_ge(hg["sq"], n + 1)
                    mm(R[:, 3, 0:T], ones[:, :], lf[:, :], start=True, stop=True).then_inc(hg["ms"], 1)

            def ml_step(j, o, n, i):
                q, k = mW[:, j, :], mW[:, 2 + j, :]
                if o == 1:
                    pe.wait_ge(ml["lr"], n + 1)
                    pe.wait_ge(ml["c2"], n + FREE)
                    pe.wait_ge(ml["c"], 4 * n + FREE)
                    mm(Rf[:, 0:512], ones8[:, :], mLR[:, 0:512], start=True, stop=True)
                    mm(Rf[:, 512:LRW], ones8[:, :], mLR[:, 512:LRW], start=True, stop=True).then_inc(ml["bc"], 1)
                    pe.wait_ge(ml["sig"], 4 * i + 2)
                    mm(R[:, 2, 0:TP], k[:, 0:P], q[:, 0:TP], start=True, stop=True)
                    mm(R[:, 2, TP:TP + P], k[:, P:TP], q[:, P:TP], start=True, stop=True)
                    mm(R[0:TS, 2, 3 * P:3 * P + TS], k[:, TP:T], q[:, TP:T], start=True, stop=True).then_inc(ml["qk"], 1)
                    for t in range(2):
                        tr(R[:, 3, P * t:P * (t + 1)], k[:, P * t:P * (t + 1)])
                    tr(R[0:TS, 3, TP:TP + P], k[:, TP:T]).then_inc(ml["kT"], 1)
                if o == 4:
                    pe.wait_ge(ml["k"], 3 * (n + 1))
                    pe.wait_ge(ml["pre"], 2 * (i + 1))
                    for t in range(2):
                        for v in range(2):
                            tr(R[:, 3, MV * t + P * v:MV * t + P * (v + 1)], mW[:, 4 + 2 * j + v, P * t:P * (t + 1)])
                    pe.wait_ge(ml["arg"], 3 * (n + 1))
                    pe.wait_ge(ml["e"], 2 * (n + 1))
                    for v in range(2):
                        x = tr(R[0:TS, 0, P * v:P * (v + 1)], mW[:, 4 + 2 * j + v, TP:T])
                    x.then_inc(ml["vT"], 1)
                if o == 6:
                    pe.wait_ge(ml["v"], 2 * (n + 1))
                    pe.wait_ge(ml["p"], 2 * (n + 1))
                    pe.wait_ge(ml["q"], 2 * (n + 1))
                    pe.wait_ge(ml["c0"], 16 * (n + 1))
                    for v in range(3):
                        bank = 1 + v
                        lhs = [mV[:, 0, P * v:P * (v + 1)], mV[:, 1, P * v:P * (v + 1)], mV[0:TS, 2, P * v:P * (v + 1)]] if v < 2 else \
                            [ones[:, :], ones[:, :], ones[0:TS, :]]
                        mm(R[:, bank, 0:TP], lhs[0], pm[:, 0:TP], start=True, stop=False, skip_group_check=True)
                        mm(R[:, bank, P:TP], lhs[1], pm[:, TP:TP + P], start=False, stop=False, skip_group_check=True)
                        mm(R[:, bank, TP:T], lhs[2], pm[0:TS, 3 * P:3 * P + TS], start=False, stop=False, skip_group_check=True)
                        if v < 2:
                            for b in range(NS):
                                x = mm(R[:, bank, TP + LS * b:TP + LS * (b + 1)], C0[:, b, P * v:P * (v + 1)], qi[:, LS * b:LS * (b + 1)], start=False, stop=b == NS - 1, skip_group_check=True)
                        else:
                            x = mm(R[:, bank, TP:T], ones[:, :], qn[:, :], start=False, stop=True, skip_group_check=True)
                    x.then_inc(ml["num"], 1)
                if o == 8:
                    pe.wait_ge(ml["sq"], n + 1)
                    for v in range(2):
                        x = mm(R[:, 0, 0:T], ones[:, :], hsq[:, v, :], start=v == 0, stop=v == 1)
                    x.then_inc(ml["ms"], 1)
                    pe.wait_ge(ml["vx"], n + 1)
                    pe.wait_ge(ml["h"], 4 * (n + 1))
                    for t in range(2):
                        mm(R[:, 1, 0:MV], mK[:, t, :], mV[:, t, :], start=t == 0, stop=t == 1)
                    for t in range(2):
                        mm(R[:, 1, MV:MV + 1], mK[:, t, :], ones[:, 0:1], start=t == 0, stop=t == 1)
                    mm(R[:, 1, MV + 1:MV + 1 + NS], mK[0:TS, 2, :], bmask[:, :], start=True, stop=True)
                    for u in range(2):
                        x = mm(R[:, 2 + u, :], mK[0:TS, 2, :], mVx[:, 2 * u:2 * u + 2, :].rearrange("p a b -> p (a b)"), start=True, stop=True)
                    x.then_inc(ml["st1"], 1)
                if o == 10:
                    pe.wait_ge(ml["c"], 4 * (n + 1) + FREE)
                    for u in range(2):
                        x = mm(R[:, 2 + u, :], mK[0:TS, 2, :], mVx[:, 4 + 2 * u:6 + 2 * u, :].rearrange("p a b -> p (a b)"), start=True, stop=True)
                    x.then_inc(ml["st2"], 1)

            stream(hg_base(0), HG_BLOCKS, A_HG)
            pe.wait_ge(row_d, ROW_T)
            pe.wait_ge(row_a, 6)
            for g in range(2):
                for t in range(3):
                    w = P if t < 2 else TS
                    x = tr(R[0:w, 0, 32 * g + MH * t:32 * g + MH * (t + 1)], merged[0:MH, 8 + 5 * g, P * t:P * t + w])
            x.then_inc(row_t, 1)
            pe.wait_ge(row_c, 6)

            with pe.Fori(0, 3) as i:
                def hook(k):
                    for j, o in HG_AT[k]:
                        hg_step(j, o, 4 * i + j, i)
                stream(hg_base(i + 1), HG_BLOCKS, A_HG + 2 + 2 * i, hook)

            def hook(k):
                for j, o in HG_AT_ML[k]:
                    hg_step(j, o, 12 + j, 3)
            stream(ml_base(0), ML_BLOCKS, A_ML, hook)
            pe.wait_ge(hg["out"], HH + FREE)
            with pe.Fori(0, 3) as i:
                def hook(k):
                    for j, o in ML_AT[k]:
                        ml_step(j, o, 2 * i + j, i)
                stream(ml_base(i + 1), ML_BLOCKS, A_ML + 4 + 4 * i, hook)

            def hook(k):
                for j, o in ML_AT_ADA[k]:
                    ml_step(j, o, 6 + j, 3)
            stream(ada2_base(0), "a" * 8, A_ADA2, hook)
            pe.wait_ge(ml["c"], 4 * MH + FREE)
            pe.wait_ge(ml["c2"], MH + FREE)
            nc.tensor.transpose(R[0:NB * MH, 1, 0:P], nnew[:].rearrange("p a b -> p (a b)"), ident[:, :]).then_inc(n_t, 1)
            stream(out_base(0), "ss", 0, xparts=4)
            with pe.Fori(1, 4) as i:
                stream(out_base(i), "ss", 0)
            pe.wait_ge(x1_acc, 3 + FREE)
            for t in range(8):
                if t == 4:
                    pe.wait_ge(x1_sq, 4)
                x = mm(R[:, 0, 0:T], ones[:, :], sqacc[:, t, :] if t < 4 else mixo[:, 8 + t, :], start=t == 0, stop=t == 7)
            x.then_inc(ms_done, 1)
            stream(up_base(0), "ss", 0, xparts=8)
            with pe.Fori(1, 22) as i:
                stream(up_base(i), "ss", 0)

            def down(i, g0=None):
                for u in range(4):
                    pe.wait_ge(bank_free[u % 2], down_base(i)[1] + u // 2 + FREE)
                    for s in range(11):
                        k = 11 * u + s
                        if isinstance(i, int) and u == 0:
                            pe.wait_ge(ff_lo, 2 * (s + 1) + FREE)
                        chunk(down_base(i)[0] + k, k, s == 0, s == 10, u % 2, ffh, ffl, KC * s)
                        if i == 0 and k % 2 == 0 and k < 22:
                            g = k // 2
                            pe.wait_ge(ab_tail, 44 + FREE)
                            if g >= 2:
                                pe.wait_ge(tl_c, g - 1)
                            for t in range(4):
                                x = tr(R[0:2 + NS * 2, 1 + g % 2, P * t:P * (t + 1)], tails[:, 4 * g + t, :])
                            x.then_inc(tl_t, 1)

            down(0)
            down(1)
            pe.wait_ge(x2_acc, 8)
            for t in range(2):
                x = mm(R[:, 0, 0:T], ones[:, :], sqf[:, t, :], start=t == 0, stop=t == 1)
            x.then_inc(ms_done, 1)
            for tt in range(3):
                w = P if tt < 2 else TS
                for g in range(4):
                    e = 4 * tt + g
                    pe.wait_ge(y_w, 4 * (g + 1))
                    if e < 3:
                        pe.wait_ge(tl_c, 11)
                    if e >= 3:
                        pe.wait_ge(y_c, e - 2)
                    for t in range(4):
                        x = tr(R[0:w, 1 + e % 3, P * t:P * (t + 1)], yT[:, 4 * g + t, P * tt:P * tt + w])
                    x.then_inc(y_t, 1)

        @block.scalar
        def _(act):
            A = nc.scalar.activation

            def hi(N, k, first=False):
                s = k % RING
                act.wait_ge(landed[s], 4 * N[0] + 16 * (k // RING + 1))
                if not first or k >= RING:
                    act.wait_ge(used, N[0] + k - 3 + FREE)
                A(whi[:, s], raw[:, s], ACT.Copy).then_inc(hi_done, 1)

            def ada_rows_of(bank):
                A(arows[:, bank, :], ps[0:2 * NB, bank, 0, 0:CN], ACT.Copy).then_inc(ada_rows, 1)

            act.sem_inc(hg["rstd"], FREE)
            act.sem_inc(x_c, X_FREE)
            act.dma_start(ctm[0:1, :], c_prompt).then_inc(ld_c, 16)
            act.dma_start(ctm[1:NB, :], c_sample).then_inc(ld_c, 16)
            for t in range(2):
                act.dma_start(xtm[:, t, :], x_prompt[0, P * t:P * (t + 1), :]).then_inc(ld_x, 16)
            act.dma_start(xtm[0:TS, 2, :], x_sample.rearrange("b t d -> (b t) d")).then_inc(ld_x, 16)

            def row128(a):
                return a.rearrange("(r c) -> r c", c=P)
            for dst, src in ((partm[0:96, 0, :], row128(ada_b[0])),
                             (partm[96:128, 0, :], hg_lb_logits.rearrange("i (r c) -> (i r) c", c=P)),
                             (partm[0:16, 1, :], row128(hg_norm_w[0])), (partm[16:32, 1, :], row128(ml_norm_w[0])),
                             (partm[32:48, 1, :], row128(final_norm_w)), (partm[48:92, 1, :], row128(conv_b[0])),
                             (partm[0:88, 2, :], conv_w[0, 0:2].rearrange("j (r c) -> (j r) c", c=P)),
                             (partm[0:44, 3, :], row128(conv_w[0, 2])),
                             (partm[44:108, 3, :], state_mlstm_n[0].rearrange("b h d -> (b h) d"))):
                act.dma_start(dst, src).then_inc(ld_par, 16)
            with nc.allow_non_contiguous_dma(reason="a few columns"):
                act.dma_start(gw[:, :, :], win_v[:, :, C_MI:C_MI + 2 * MH]).then_inc(ld_gw, 16)
                act.dma_start(gb[:, 0:1], ml_i_bias.rearrange("a h -> h a")).then_inc(ld_gs, 16)
                act.dma_start(gb[:, 1:2], ml_f_bias.rearrange("a h -> h a")).then_inc(ld_gs, 16)
                act.dma_start(m0[:, :], state_mlstm_m[0].rearrange("b h -> h b")).then_inc(ld_gs, 16)
            act.dma_start(cvr[:, :], state_conv[0].rearrange("b j f -> (b j) f")).then_inc(ld_conv, 16)

            act.wait_ge(ld_c, 32)
            A(ctm[:, :], ctm[:, :], ACT.Silu).then_inc(c_silu, 1)
            act.wait_ge(c_t, 1)
            A(cT[:, :, :], R[:, 3, 0:KT * NB].rearrange("p (k b) -> p k b", b=NB), ACT.Copy).then_inc(c_c, 1)
            act.wait_ge(c_c, 1)
            A(cs[:, :, 0:NB], cT[:, :, :], ACT.Copy).then_inc(c_hi, 1)
            act.wait_ge(par_t, 1)
            A(par[:, 0, :], R[:, 2, 0:P], ACT.Copy)
            A(par[:, 1, 0:92], R[:, 2, P:P + 92], ACT.Copy)
            A(par[:, 2, 0:88], R[:, 2, 2 * P:2 * P + 88], ACT.Copy)
            A(par[:, 3, 0:108], R[:, 2, 3 * P:3 * P + 108], ACT.Copy).then_inc(par_c, 1)
            def root(nth, src, scale):
                act.wait_ge(ms_done, nth)
                if nth > 1:
                    act.wait_ge(xn_done, 4 * (nth - 1))
                A(lnms[:, :], src, ACT.Ln, bias=epsc[:, 0:1], scale=scale).then_inc(rs_done, 1)
                act.wait_ge(rs_done, 2 * nth - 1)
                A(rstd[:, :], lnms[:, :], ACT.Exp, scale=-0.5).then_inc(rs_done, 1)

            def modulate(nth, tmp, shift, scale):
                act.wait_ge(sc_one, nth)
                for g in range(4):
                    act.wait_ge(xn_done, 4 * (nth - 1) + g + 1)
                    for kt in range(4 * g, 4 * g + 4):
                        x = A(tmp[:, kt, 0:TP], tmp[:, kt, 0:TP], ACT.Identity, bias=mod[:, shift + kt, 0:1], scale=mod[:, scale + kt, 0:1])
                    x.then_inc(md_p, 1)
                    act.wait_ge(md_p, 4 * (nth - 1) + g + 1)
                    act.wait_ge(md_s, 2 * (4 * (nth - 1) + g + 1))
                    if g == 0 and nth == 2:
                        act.wait_ge(used, N_UP[0] + FREE)
                    A(xh[:, 4 * g:4 * g + 4, :], tmp[:, 4 * g:4 * g + 4, :], ACT.Copy).then_inc(xhi, 1)

            def ada1(i, with_x, first=False):
                for k in range(8):
                    hi(ada1_base(i), k + LEAD, first=first)
                    if k % 4 == 3:
                        act.wait_ge(used, ada1_base(i)[0] + k + 1 + FREE)
                        ada_rows_of(k // 4)
                    if with_x and k % 2:
                        j = k // 2
                        act.wait_ge(x_t, 4 * i + j + 1)
                        A(xT[:, bass.ds(4 * i + j, 1), :].rearrange("p a b -> p (a b)"), R[:, j % 2, 0:T], ACT.Copy).then_inc(x_c, 1)
                if with_x:
                    act.wait_ge(x_c, 4 * (i + 1) + X_FREE)
                    A(merged[:, bass.ds(4 * i, 4), :], xT[:, bass.ds(4 * i, 4), :], ACT.Square).then_inc(sq_done, 1)

            for k in range(LEAD):
                hi(N_ADA1, k, first=True)
            ada1(0, True, first=True)
            with act.Fori(1, 4) as i:
                ada1(i, True)
            act.wait_ge(lb_d, 3)
            A(lbc[:, :, :], lbc[:, :, :], ACT.Exp).then_inc(lb_a, 1)
            act.wait_ge(ld_gw, 16)
            A(gwh[:, :, :], gw[:, :, :], ACT.Copy).then_inc(gw_hi, 1)
            for g in range(2):
                act.wait_ge(cv_t, g + 1)
                A(cst[:, 22 * g:22 * g + 22, :], R[:, 2 + g, 0:352].rearrange("p (f r) -> p f r", r=16), ACT.Copy).then_inc(cv_c, 1)
            act.wait_ge(const, 6)
            root(1, R[:, 0, 0:T], 1.0 / D)
            with act.Fori(4, 8) as i:
                ada1(i, False)
            modulate(1, merged, 0, KT)
            r = merged[0:MH]
            act.wait_ge(gmm, 1)
            act.wait_ge(ld_gs, 48)
            act.wait_ge(xlo, 4)
            A(r[:, 0, :], R[0:MH, 0, 0:T], ACT.Identity, bias=gb[:, 0:1]).then_inc(row_a, 1)
            A(r[:, 1, :], R[0:MH, 1, 0:T], ACT.Identity, bias=gb[:, 1:2]).then_inc(row_a, 1)
            act.wait_ge(row_a, 2)
            A(r[:, 2, :], r[:, 1, :], ACT.Abs).then_inc(row_a, 1)
            act.wait_ge(row_a, 3)
            A(r[:, 3, :], r[:, 2, :], ACT.Exp, scale=-1.0).then_inc(row_a, 1)
            act.wait_ge(row_a, 4)
            A(r[:, 4, :], r[:, 3, :], ACT.Ln, bias=onec[0:MH, 0:1]).then_inc(row_a, 1)
            act.wait_ge(row_d, ROW_WK)
            A(r[:, 13, :], r[:, 12, :], ACT.Exp).then_inc(row_a, 1)

            def stream(N, kinds, dst, hook):
                for b, kind in enumerate(kinds):
                    for s in range(4):
                        k = 4 * b + s
                        hi(N, k + LEAD)
                        if s == 3:
                            act.wait_ge(used, N[0] + k + 1 + FREE)
                            if kind == "s":
                                A(dst(b - ada_before(b, kinds)), ps[:, b % 2, :, 0:T], ACT.Copy).then_inc(bank_free[b % 2], 1)
                            else:
                                ada_rows_of(b % 2)
                        hook(k)

            def hg_block(i):
                def dst(u):
                    if i is not None and u == 0:
                        act.wait_ge(hg["sig"], 4 * (i + 1))
                    if i is not None and u == 4:
                        act.wait_ge(hg["pre"], 2 * (i + 1))
                    return S[:, u // 2, 2 * (u % 2):2 * (u % 2) + 2, :]
                return dst

            def hg_prologue(k, i):
                if k == 0:
                    for p in range(2):
                        act.wait_ge(bank_free[p], hg_base(i + 1)[1] + FREE)
                    act.wait_ge(hg["out"], 4 * i + FREE)
                    A(W[:, 1], S[:, 1], ACT.Sigmoid, scale=-1.0).then_inc(hg["sig"], 1)
                    A(W[:, 4], S[:, 4], ACT.Sigmoid).then_inc(hg["sig"], 1)
                if k == 1:
                    A(W[:, 0], S[:, 0], ACT.Silu).then_inc(hg["sig"], 1)
                    A(W[:, 3], S[:, 3], ACT.Silu).then_inc(hg["sig"], 1)

            def hg_step(j, o, n, i):
                h = n
                if o == 0:
                    act.wait_ge(hg["sig"], 4 * (i + 1))
                    A(lf[:, :], W[:, 1, j, :], ACT.Ln, bias=onec[:, 0:1], scale=lbc[:, 0, bass.ds(h, 1)]).then_inc(hg["logf"], 1)
                if o == 1:
                    act.wait_ge(hg["bm"], 2 * (n + 1))
                    act.wait_ge(hg["out"], n + FREE)
                    A(e1[:, :], bm[:, :], ACT.Exp).then_inc(hg["exp"], 1)
                    A(e2[:, :], bm[:, :], ACT.Exp, scale=-1.0).then_inc(hg["exp"], 1)
                    A(er[:, :], seq(bc[:, 0:TP], SUB)[:, :, SUB // 2 - 1], ACT.Exp).then_inc(hg["exp"], 1)
                if o == 3:
                    act.wait_ge(hg["tr"], 2 * (n + 1))
                    A(Vt[:, :, :], R[:, 1, 0:TP].rearrange("p (a b) -> p a b", a=2), ACT.Copy).then_inc(hg["tok"], 1)
                    A(Vts[:, :], R[0:TS, 1, TP:TP + P], ACT.Copy).then_inc(hg["tok"], 1)
                    A(Kt[:, :, :], R[:, 2, 0:TP].rearrange("p (a b) -> p a b", a=2), ACT.Copy).then_inc(hg["tok"], 1)
                    A(Kts[:, :], R[0:TS, 2, TP:TP + P], ACT.Copy).then_inc(hg["tok"], 1)
                if o == 7:
                    act.wait_ge(hg["o"], n + 1)
                    A(lf[:, :], R[:, 2, 0:T], ACT.Square).then_inc(hg["sq"], 1)
                if o == 8:
                    act.wait_ge(hg["ms"], n + 1)
                    A(bc[:, :], R[:, 3, 0:T], ACT.Ln, bias=epsc[:, 0:1], scale=1.0 / P).then_inc(hg["rstd"], 1)
                    act.wait_ge(hg["rstd"], 2 * n + 1 + FREE)
                    A(e2[:, :], bc[:, :], ACT.Exp, scale=-0.5).then_inc(hg["rstd"], 1)

            def ml_block(i):
                def dst(u):
                    if i is not None:
                        act.wait_ge(ml["pre"], 2 * (i + 1))
                    return mS[:, 2 * u:2 * u + 2, :]
                return dst

            def ml_prologue(k, i):
                if k == 0:
                    for p in range(2):
                        act.wait_ge(bank_free[p], ml_base(i + 1)[1] + FREE)
                    act.wait_ge(ml["out"], 4 * i + FREE)
                    A(mW[:, 0:2, :], mS[:, 0:2, :], ACT.Copy, scale=HSC).then_inc(ml["sig"], 1)
                    A(mW[:, 2:4, :], mS[:, 2:4, :], ACT.Copy).then_inc(ml["sig"], 1)
                if k == 1:
                    A(mW[:, 8:12, :], mS[:, 8:12, :], ACT.Sigmoid).then_inc(ml["sig"], 1)
                    A(mS[:, 12:16, :], mS[:, 12:16, :], ACT.Sigmoid).then_inc(ml["sig"], 1)

            def ml_step(j, o, n, i):
                h = n
                if o == 2:
                    act.wait_ge(ml["kT"], n + 1)
                    for t in range(3):
                        w = P if t < 2 else TS
                        A(mK[0:w, t, :], R[0:w, 3, P * t:P * (t + 1)], ACT.Copy, scale=wkcol[0:w, t, bass.ds(h, 1)]).then_inc(ml["k"], 1)
                    act.wait_ge(ml["arg"], 3 * (n + 1))
                    A(em[:, :], Rf[:, T:2 * T], ACT.Exp).then_inc(ml["e"], 1)
                    A(es[:, :], Rf[:, 2 * T:LRW], ACT.Exp).then_inc(ml["e"], 1)
                if o == 3:
                    act.wait_ge(ml["arg"], 3 * (n + 1))
                    for t, (w, a, b) in enumerate(((P, 0, TP), (P, TP, 3 * P), (TS, 3 * P, 3 * P + TS))):
                        A(dx[0:w, a:b], arg[0:w, a:b], ACT.Exp, bias=acol[0:w, t, bass.ds(h, 1)]).then_inc(ml["d"], 1)
                if o == 5:
                    act.wait_ge(ml["vT"], n + 1)
                    A(mV[:, 0:2, :], R[:, 3, :].rearrange("p (a b) -> p a b", a=2), ACT.Copy).then_inc(ml["v"], 1)
                    A(mV[0:TS, 2, :], R[0:TS, 0, 0:MV], ACT.Copy).then_inc(ml["v"], 1)
                if o == 7:
                    act.wait_ge(ml["num"], n + 1)
                    A(dn[:, :], R[:, 3, 0:T], ACT.Abs).then_inc(ml["dn"], 1)
                if o == 8:
                    act.wait_ge(ml["h"], 4 * (n + 1))
                    A(hsq[:, :, :], hh[:, :, :], ACT.Square).then_inc(ml["sq"], 1)
                if o == 9:
                    act.wait_ge(ml["ms"], n + 1)
                    A(em[:, :], R[:, 0, 0:T], ACT.Ln, bias=epsc[:, 0:1], scale=1.0 / MV).then_inc(ml["r"], 1)
                    act.wait_ge(ml["r"], 2 * n + 1)
                    A(dn[:, :], em[:, :], ACT.Exp, scale=-0.5).then_inc(ml["r"], 1)

            act.wait_ge(ml["st"], 32)
            stream(hg_base(0), HG_BLOCKS, hg_block(None), lambda k: None)
            act.wait_ge(row_t, 1)
            for g, dst in ((0, acol), (1, wkcol)):
                for t in range(3):
                    w = P if t < 2 else TS
                    A(dst[0:w, t, :], R[0:w, 0, 32 * g + MH * t:32 * g + MH * (t + 1)], ACT.Copy).then_inc(row_c, 1)
            with act.Fori(0, 3) as i:
                def hook(k):
                    hg_prologue(k, i)
                    for j, o in HG_AT[k]:
                        hg_step(j, o, 4 * i + j, i)
                stream(hg_base(i + 1), HG_BLOCKS, hg_block(i), hook)

            def hook(k):
                hg_prologue(k, 3)
                for j, o in HG_AT_ML[k]:
                    hg_step(j, o, 12 + j, 3)

            def first_ml_block(u):
                act.wait_ge(hg["pre"], 2 * 4)
                return mS[:, 2 * u:2 * u + 2, :]
            stream(ml_base(0), ML_BLOCKS, first_ml_block, hook)
            act.wait_ge(hg["out"], HH + FREE)
            with act.Fori(0, 2) as i:
                def hook(k):
                    ml_prologue(k, i)
                    for j, o in ML_AT[k]:
                        ml_step(j, o, 2 * i + j, i)
                stream(ml_base(i + 1), ML_BLOCKS, ml_block(i), hook)

            def hook(k):
                ml_prologue(k, 2)
                for j, o in ML_AT[k]:
                    ml_step(j, o, 4 + j, 2)
            stream(ml_base(3), ML_BLOCKS, ml_block(2), hook)

            def hook(k):
                ml_prologue(k, 3)
                for j, o in ML_AT_ADA[k]:
                    ml_step(j, o, 6 + j, 3)
            stream(ada2_base(0), "a" * 8, None, hook)
            act.wait_ge(n_t, 1)
            A(ntok[:, :], R[0:NB * MH, 1, 0:P], ACT.Copy).then_inc(n_c, 1)
            act.wait_ge(ml["out"], 2 * MH + FREE)
            act.wait_ge(used, N_ADA2[0] + FREE)
            for g in range(4):
                A(xh[:, 4 * g:4 * g + 4, :], merged[:, 4 * g:4 * g + 4, :], ACT.Copy).then_inc(xhi, 1)
            with act.Fori(0, 4) as i:
                for k in range(8):
                    hi(out_base(i), k + LEAD)
                act.wait_ge(x1_a, 2 * (i + 1))
                A(mixo[:, bass.ds(4 * i, 4), :], xT2[:, bass.ds(4 * i, 4), :], ACT.Square).then_inc(x1_sq, 1)
            root(2, R[:, 0, 0:T], 1.0 / D)
            modulate(2, mixo, 3 * KT, 4 * KT)
            act.wait_ge(spill_1, 16)
            with act.Fori(0, 22) as i:
                for k in range(8):
                    hi(up_base(i), k + LEAD)
                    if k == 3:
                        act.wait_ge(used, up_base(i)[0] + 4 + FREE)
                        act.wait_ge(ff_conv, 6 * i + FREE)
                        act.wait_ge(ab_tail, 2 * i + FREE)
                        A(abuf[:, :, 2:2 + TP], ps[:, 0, :, 0:TP], ACT.Copy).then_inc(ab_ready, 1)
                        A(seq3(abuf[:, :, 2 + TP:AB], 2 + LS)[:, :, :, 2:2 + LS], seq3(ps[:, 0, :, TP:T], LS), ACT.Copy).then_inc(bank_free[0], 1)
                    if k == 5:
                        act.wait_ge(ff_conv, 6 * (i + 1) + FREE)
                        A(acv[:, :, 0:AB - 2], acv[:, :, 0:AB - 2], ACT.Gelu).then_inc(ff_gelu, 1)
                    if k == 7:
                        act.wait_ge(bank_free[1], N_UP[1] + i + 1 + FREE)
                        A(ffh[:, bass.ds(2 * i, 2), :], yb[:, :, :], ACT.Copy).then_inc(ff_hi, 1)

            def down(i):
                for k in range(44):
                    if i == 0 or k + LEAD < 44:
                        hi(down_base(i), k + LEAD)
                    if i == 0 and k % 2 == 1 and k < 22:
                        g = k // 2
                        act.wait_ge(tl_t, g + 1)
                        if g >= 2:
                            act.wait_ge(st_cv[g % 2], 32 * (g // 2))
                        A(cts[:, g % 2, :], R[0:2 + NS * 2, 1 + g % 2, :], ACT.Copy).then_inc(tl_c, 1)
                    if k % 11 == 10:
                        b = 4 * i + k // 11
                        act.wait_ge(x2_a, b + 1)
                        if b >= 1:
                            act.wait_ge(x2_acc, b)
                        A(sqd[:, :, :], x1f[:, 2 * b:2 * b + 2, :], ACT.Square).then_inc(x2_sq, 1)
            down(0)
            down(1)
            root(3, R[:, 0, 0:T], 1.0 / D)
            for e in range(0, 12, 2):
                act.wait_ge(y_t, e + 1)
                if e:
                    act.wait_ge(y_c, e)
                w = P if e < 8 else TS
                A(ytm[0:w, e // 4, 512 * (e % 4):512 * (e % 4) + 512], R[0:w, 1 + e % 3, :], ACT.Copy).then_inc(y_c, 1)

        @block.vector
        def _(dve):
            TT, TSC, STT = nc.vector.tensor_tensor, nc.vector.tensor_scalar, nc.vector.scalar_tensor_tensor

            def lo(N, k):
                s = k % RING
                dve.wait_ge(hi_done, N[0] + k + 1)
                TT(wlo[:, s], raw[:, s], whi[:, s].bitcast(F32), ALU.subtract).then_inc(lo_done, 1)

            for s in (bank_free[0], bank_free[1], hg["snew"], hg["y"], ml["c"], ml["c2"], ff_conv, ff_lo):
                dve.sem_inc(s, FREE)
            dve.wait_ge(c_hi, 1)
            TT(cs[:, :, NB:2 * NB], cT[:, :, :], cs[:, :, 0:NB].bitcast(F32), ALU.subtract).then_inc(c_lo, 1)
            dve.wait_ge(par_c, 1)
            lg = par[:, 0, 96:128].rearrange("p (i h) -> p i h", i=2)
            TT(lbt[:, 0, :], lg[:, 0, :], lg[:, 1, :], ALU.max).then_inc(lb_d, 1)
            dve.wait_ge(lb_d, 1)
            TT(lbc[:, 0, :], lg[:, 0, :], lbt[:, 0, :], ALU.subtract).then_inc(lb_d, 1)
            TT(lbc[:, 1, :], lg[:, 1, :], lbt[:, 0, :], ALU.subtract).then_inc(lb_d, 1)
            def ada_block(n, bank, mt):
                dve.wait_ge(ada_cols, n + 1)
                TT(mod[:, bass.ds(mt, 2), :], ps[:, bank, 1, 0:2 * NB].rearrange("p (m b) -> p m b", b=NB),
                   rep_last(bias_row[:, bass.ds(mt, 2)], NB), ALU.add).then_inc(bank_free[bank], 1)

            def stream(N, kinds, A0, hook):
                for b, kind in enumerate(kinds):
                    for s in range(4):
                        k = 4 * b + s
                        lo(N, k + LEAD)
                        if s == 1 and b and kinds[b - 1] == "a":
                            n = A0 + ada_before(b - 1, kinds)
                            ada_block(n, (b - 1) % 2, 2 * n)
                        hook(k)
                if kinds[-1] == "a":
                    n = A0 + ada_before(len(kinds) - 1, kinds)
                    ada_block(n, (len(kinds) - 1) % 2, 2 * n)

            for k in range(LEAD):
                lo(N_ADA1, k)
            with dve.Fori(0, 4) as i:
                stream(ada1_base(i), "aa", 2 * i, lambda k: None)
            dve.wait_ge(lb_a, 1)
            lsum, lrec = lbt[:, 0, :], lbt[:, 1, :]
            TT(lsum, lbc[:, 0, :], lbc[:, 1, :], ALU.add).then_inc(lb_d, 1)
            dve.wait_ge(lb_d, 4)
            nc.vector.reciprocal(lrec, lsum).then_inc(lb_d, 1)
            dve.wait_ge(lb_d, 5)
            TT(lsum, lbc[:, 0, :], lrec, ALU.mult).then_inc(lb_d, 1)
            dve.wait_ge(lb_d, 6)
            TSC(lbc[:, 0, :], lsum, 1.0, None, ALU.subtract).then_inc(lb_d, 1)
            TSC(lbc[:, 1, :], lsum, -1.0, 1.0, ALU.mult, ALU.add).then_inc(lb_d, 1)
            dve.wait_ge(gw_hi, 1)
            TT(gwl[:, :, :], gw[:, :, :], gwh[:, :, :].bitcast(F32), ALU.subtract).then_inc(gw_lo, 1)

            with dve.Fori(4, 8) as i:
                stream(ada1_base(i), "aa", 2 * i, lambda k: None)

            def modulate(nth, src, tmp, shift, scale):
                dve.wait_ge(rs_done, 2 * nth)
                for p in range(2):
                    dve.wait_ge(bank_free[p], (N_HG[1] if nth == 1 else N_UP[1]) + FREE)
                TSC(mod[:, scale:scale + KT, :], mod[:, scale:scale + KT, :], 1.0, None, ALU.add).then_inc(sc_one, 1)
                dve.wait_ge(sc_one, nth)
                def parts(g):
                    dve.wait_ge(xhi, 4 * (nth - 1 if nth == 1 else 2) + g + 1)
                    TT(xl[:, 4 * g:4 * g + 4, :], tmp[:, 4 * g:4 * g + 4, :], xh[:, 4 * g:4 * g + 4, :].bitcast(F32), ALU.subtract).then_inc(xlo, 1)

                for g in range(4):
                    a, b = 4 * g, 4 * g + 4
                    m = 4 * (nth - 1) + g
                    TT(tmp[:, a:b, :], src[:, a:b, :], mid(rstd[:, :], 4), ALU.mult).then_inc(xn_done, 1)
                    dve.wait_ge(xn_done, m + 1)
                    v = seq3(tmp[:, a:b, TP:T], LS)
                    TT(v, v, rep3(mod[:, scale + a:scale + b, 1:NB], LS), ALU.mult).then_inc(md_s, 1)
                    dve.wait_ge(md_s, 2 * m + 1)
                    TT(v, v, rep3(mod[:, shift + a:shift + b, 1:NB], LS), ALU.add).then_inc(md_s, 1)
                    if g >= 2:
                        parts(g - 2)
                parts(2)
                parts(3)

            modulate(1, xT, merged, 0, KT)
            r = merged[0:MH]
            cnt = [0]

            def row(ins):
                cnt[0] += 1
                ins.then_inc(row_d, 1)
                dve.wait_ge(row_d, cnt[0])
            dve.wait_ge(row_a, 5)
            dve.wait_ge(const, CONST_ALL)
            row(TSC(r[:, 5, :], r[:, 1, :], 0.0, None, ALU.min))
            row(TT(r[:, 6, :], r[:, 5, :], r[:, 4, :], ALU.subtract))
            row(nc.vector.tensor_tensor_scan(r[:, 7, :], reset8[:, 0, :], r[:, 6, :], 0.0, ALU.mult, ALU.add))
            row(TT(r[:, 8, :], r[:, 0, :], r[:, 7, :], ALU.subtract))
            row(nc.vector.tensor_copy(r[:, 9, :], r[:, 8, :]))
            row(TSC(r[:, 9, 0:1], r[:, 8, 0:1], 0.0, None, ALU.max))
            row(TT(seq(r[:, 9, TP:T], LS)[:, :, 0], seq(r[:, 8, TP:T], LS)[:, :, 0], m0[:, :], ALU.max))
            row(nc.vector.tensor_tensor_scan(r[:, 10, :], reset8[:, 1, :], r[:, 9, :], 0.0, ALU.add, ALU.max))
            row(TSC(LR[:, 0:T], r[:, 10, :], -1.0, None, ALU.mult))
            row(TT(LR[:, T:2 * T], LR[:, 0:T], r[:, 7, :], ALU.subtract))
            nM = seq(LR[:, TP:T], LS)
            row(TT(seq(LR[:, 2 * T:2 * T + TS], LS), nM, rep_last(m0[:, :], LS), ALU.add))
            row(TT(LR[:, 2 * T + TS:LRW], nM[:, :, LS - 1], m0[:, :], ALU.add))
            row(TSC(r[:, 11, 0:1], LR[:, T + TP - 1:T + TP], -1.0, None, ALU.mult))
            row(TSC(r[:, 11, 1:NB], seq(LR[:, T + TP:2 * T], LS)[:, :, LS - 1], -1.0, None, ALU.mult))
            row(TSC(r[:, 12, 0:TP], r[:, 8, 0:TP], LR[:, TP - 1:TP], None, ALU.add))
            row(TT(seq(r[:, 12, TP:T], LS), seq(r[:, 8, TP:T], LS), nM[:, :, LS - 1:LS].to_broadcast([MH, NS, LS]), ALU.add))
            assert cnt[0] == ROW_WK == ROW_T

            def hg_step(j, o, n, i):
                h = n
                if o == 0:
                    dve.wait_ge(hg["logf"], n + 1)
                    dve.wait_ge(lb_d, 8)
                    nc.vector.tensor_tensor_scan(bc[:, :], reset[:, :], lf[:, :], 0.0, ALU.mult, ALU.add).then_inc(hg["b"], 1)
                    dve.wait_ge(hg["b"], n + 1)
                    v = seq(bc[:, 0:TP], SUB)
                    TT(seq(bm[:, 0:TP], SUB), v, v[:, :, SUB // 2 - 1:SUB // 2].to_broadcast([P, NSUB, SUB]), ALU.subtract).then_inc(hg["bm"], 1)
                    nc.vector.tensor_copy(bm[:, TP:T], bc[:, TP:T]).then_inc(hg["bm"], 1)
                if o == 1:
                    dve.wait_ge(hg["exp"], 3 * (n + 1))
                    dve.wait_ge(hg["sig"], 4 * (i + 1))
                    STT(qt[:, :], W[:, 0, j, :], HSC, e1[:, :], ALU.mult, ALU.mult).then_inc(hg["qk"], 1)
                    STT(kt_[:, :], W[:, 1, j, :], lbc[:, 1, bass.ds(h, 1)], e2[:, :], ALU.mult, ALU.mult).then_inc(hg["qk"], 1)
                if o == 3:
                    count = known(dve, n + 1)
                    dve.wait_ge(const, CONST_ALL)
                    dve.wait_ge(hg["scores"], count)
                    nc.vector.copy_predicated(PT[:, :, :], mid(hmask[:, :], 2), R[:, 0, 0:TP].rearrange("p (a b) -> p a b", a=2)).then_inc(hg["pt"], 1)
                    nc.vector.copy_predicated(PTs[:, :], hmask_s[:, :], R[0:TS, 0, TP:T]).then_inc(hg["pt"], 1)
                if o == 5:
                    dve.wait_ge(hg["u"], 2 * (n + 1))
                    dve.wait_ge(hg["dk"], 4 * (n + 1))
                    dve.wait_ge(hg["st"], 32 * (n + 1))
                    nc.vector.tensor_copy(Sst[:, 0, :], R[:, 3, 0:P]).then_inc(hg["state"], 1)
                    for c in range(1, NSUB):
                        dve.wait_ge(hg["state"], 8 * n + c)
                        STT(Sst[:, c, :], Sst[:, c - 1, :], dec[:, c:c + 1], R[:, 3 if c < 4 else 1, P * (c % 4):P * (c % 4 + 1)], ALU.mult, ALU.add).then_inc(hg["state"], 1)
                if o == 7:
                    dve.wait_ge(hg["us"], n + 1)
                    dve.wait_ge(hg["scaled"], n + 1)
                    TT(S0[:].rearrange("p a b -> p (a b)"), S0[:].rearrange("p a b -> p (a b)"), Rf[:, 0:1024], ALU.add).then_inc(hg["snew"], 1)
                if o == 8:
                    dve.wait_ge(hg["rstd"], 2 * (n + 1) + FREE)
                    STT(e1[:, :], R[:, 2, 0:T], par[:, 1, bass.ds(h, 1)], e2[:, :], ALU.mult, ALU.mult).then_inc(hg["y"], 1)

            def ml_step(j, o, n, i):
                h = n
                if o == 0:
                    dve.wait_ge(ml["bc"], n + FREE)
                    TSC(mLR[:, :], LR[:, :], ident[0:MH, bass.ds(h, 1)], None, ALU.mult).then_inc(ml["lr"], 1)
                if o == 2:
                    dve.wait_ge(ml["bc"], n + 1 + FREE)
                    TT(arg[:, 0:TP], R[:, 0, 0:TP], amask[:, :], ALU.add).then_inc(ml["arg"], 1)
                    TT(arg[:, TP:3 * P], R[:, 0, P:TP], amask[:, 0:P], ALU.add).then_inc(ml["arg"], 1)
                    TT(arg[0:TS, 3 * P:3 * P + TS], R[0:TS, 0, TP:T], amask_s[:, :], ALU.add).then_inc(ml["arg"], 1)
                if o == 4:
                    dve.wait_ge(ml["d"], 3 * (n + 1))
                    dve.wait_ge(ml["qk"], n + 1)
                    dve.wait_ge(ml["e"], 2 * (n + 1))
                    TT(pm[:, 0:3 * P], dx[:, 0:3 * P], R[:, 2, 0:3 * P], ALU.mult).then_inc(ml["p"], 1)
                    TT(pm[0:TS, 3 * P:3 * P + TS], dx[0:TS, 3 * P:3 * P + TS], R[0:TS, 2, 3 * P:3 * P + TS], ALU.mult).then_inc(ml["p"], 1)
                    TT(qi[:, :], mW[:, j, TP:T], es[:, 0:TS], ALU.mult).then_inc(ml["q"], 1)
                    dve.wait_ge(ml["q"], 2 * n + 1)
                    TT(seq(qn[:, :], LS), seq(qi[:, :], LS), n0v[:, :, bass.ds(h, 1)].to_broadcast([P, NS, LS]), ALU.mult).then_inc(ml["q"], 1)
                if o == 7:
                    dve.wait_ge(ml["dn"], n + 1)
                    dve.wait_ge(ml["out"], 2 * n + FREE)
                    TT(dn[:, :], dn[:, :], em[:, :], ALU.max).then_inc(ml["h"], 1)
                    dve.wait_ge(ml["h"], 4 * n + 1)
                    nc.vector.reciprocal(dn[:, :], dn[:, :]).then_inc(ml["h"], 1)
                    dve.wait_ge(ml["h"], 4 * n + 2)
                    for v in range(2):
                        TT(hh[:, v, :], R[:, 1 + v, 0:T], dn[:, :], ALU.mult).then_inc(ml["h"], 1)
                if o == 9:
                    dve.wait_ge(ml["r"], 2 * (n + 1))
                    for v in range(2):
                        STT(hh[:, v, :], hh[:, v, :], mlw[:, v, bass.ds(h, 1)], dn[:, :], ALU.mult, ALU.mult).then_inc(ml["y"], 1)
                    dve.wait_ge(ml["st1"], n + 1)
                    dve.wait_ge(ml["cs"], 2 * (n + 1))
                    dve.wait_ge(ml["st"], 32 * (n + 1))
                    TT(C0[:, 0:4, :].rearrange("p a b -> p (a b)"), C0[:, 0:4, :].rearrange("p a b -> p (a b)"), Rf[:, 1024:2048], ALU.add).then_inc(ml["c"], 1)
                    nc.vector.tensor_copy(Cp[:, :], R[:, 1, 0:MV]).then_inc(ml["c"], 1)
                    nc.vector.tensor_copy(nnew[:, 0, bass.ds(h, 1)], R[:, 1, MV:MV + 1]).then_inc(ml["c"], 1)
                    TT(nnew[:, 1:NB, bass.ds(h, 1)], ndec[:, :].rearrange("p (b a) -> p b a", a=1), R[:, 1, MV + 1:MV + 1 + NS].rearrange("p (b a) -> p b a", a=1), ALU.add).then_inc(ml["c"], 1)
                if o == 11:
                    dve.wait_ge(ml["st2"], n + 1)
                    TT(C0[:, 4:8, :].rearrange("p a b -> p (a b)"), C0[:, 4:8, :].rearrange("p a b -> p (a b)"), Rf[:, 1024:2048], ALU.add).then_inc(ml["c2"], 1)

            n0v = par[:, 3, 44:108].rearrange("p (b h) -> p b h", h=MH)
            mlw = par[:, 1, 16:32].rearrange("p (h v) -> p v h", v=2)

            stream(hg_base(0), HG_BLOCKS, A_HG, lambda k: None)
            dve.wait_ge(hg["zero"], 3)
            with dve.Fori(0, 3) as i:
                def hook(k):
                    for j, o in HG_AT[k]:
                        hg_step(j, o, 4 * i + j, i)
                stream(hg_base(i + 1), HG_BLOCKS, A_HG + 2 + 2 * i, hook)

            def hook(k):
                for j, o in HG_AT_ML[k]:
                    hg_step(j, o, 12 + j, 3)
            stream(ml_base(0), ML_BLOCKS, A_ML, hook)
            dve.wait_ge(hg["out"], HH + FREE)
            dve.wait_ge(hg["st"], 32 * (HH + 1))
            with dve.Fori(0, 2) as i:
                def hook(k):
                    for j, o in ML_AT[k]:
                        ml_step(j, o, 2 * i + j, i)
                stream(ml_base(i + 1), ML_BLOCKS, A_ML + 4 + 4 * i, hook)

            def hook(k):
                for j, o in ML_AT[k]:
                    ml_step(j, o, 4 + j, 2)
            stream(ml_base(3), ML_BLOCKS, A_ML + 12, hook)

            def hook(k):
                for j, o in ML_AT_ADA[k]:
                    ml_step(j, o, 6 + j, 3)
            stream(ada2_base(0), "a" * 8, A_ADA2, hook)
            for g in range(4):
                dve.wait_ge(xhi, 4 + g + 1)
                TT(xl[:, 4 * g:4 * g + 4, :], merged[:, 4 * g:4 * g + 4, :], xh[:, 4 * g:4 * g + 4, :].bitcast(F32), ALU.subtract).then_inc(xlo, 1)
            dve.wait_ge(back_x, 16)
            with dve.Fori(0, 4) as i:
                for k in range(8):
                    lo(out_base(i), k + LEAD)
                    if k % 4 == 3:
                        b = k // 4
                        kt = bass.ds(4 * i + 2 * b, 2)
                        g1 = mod[:, bass.ds(2 * KT + 4 * i + 2 * b, 2), :]
                        dve.wait_ge(used, out_base(i)[0] + k + 1 + FREE)
                        TT(mixo[:, kt, 0:TP], ps[:, b, :, 0:TP], g1[:, :, 0:1].to_broadcast([P, 2, TP]), ALU.mult).then_inc(x1_m, 1)
                        TT(seq3(mixo[:, kt, TP:T], LS), seq3(ps[:, b, :, TP:T], LS), rep3(g1[:, :, 1:NB], LS), ALU.mult).then_inc(bank_free[b], 1)
                        dve.wait_ge(bank_free[b], N_OUT[1] + i + 1 + FREE)
                        TT(xT2[:, kt, :], xT2[:, kt, :], mixo[:, kt, :], ALU.add).then_inc(x1_a, 1)
            modulate(2, xT2, mixo, 3 * KT, 4 * KT)
            dve.wait_ge(zab, 2)
            dve.wait_ge(spill_1, 16)
            cb = par[:, 1, 48:92]
            cw = [par[:, 2, 0:44], par[:, 2, 44:88], par[:, 3, 0:44]]
            with dve.Fori(0, 22) as i:
                for k in range(8):
                    lo(up_base(i), k + LEAD)
                    if k == 4:
                        dve.wait_ge(bank_free[0], N_UP[1] + i + 1 + FREE)
                        dve.wait_ge(ab_lead, i + 1)
                        for m in range(2):
                            c1 = bass.ds(2 * i + m, 1)
                            TSC(acv[:, m, 0:AB - 2], abuf[:, m, 0:AB - 2], cw[0][:, c1], cb[:, c1], ALU.mult, ALU.add).then_inc(ff_conv, 1)
                        for w in (1, 2):
                            for m in range(2):
                                c1 = bass.ds(2 * i + m, 1)
                                dve.wait_ge(ff_conv, 6 * i + 2 * (w - 1) + m + 1 + FREE)
                                STT(acv[:, m, 0:AB - 2], abuf[:, m, w:w + AB - 2], cw[w][:, c1], acv[:, m, 0:AB - 2], ALU.mult, ALU.add).then_inc(ff_conv, 1)
                    if k == 7:
                        dve.wait_ge(used, up_base(i)[0] + 8 + FREE)
                        dve.wait_ge(ff_gelu, i + 1)
                        dve.wait_ge(ff_lo, i + FREE)
                        TT(yb[:, :, 0:TP], acv[:, :, 0:TP], ps[:, 1, :, 0:TP], ALU.mult).then_inc(ff_y, 1)
                        for m in range(2):
                            x = TT(seq(yb[:, m, TP:T], LS), seq(acv[:, m, 2 + TP:AB], 2 + LS)[:, :, 0:LS], seq(ps[:, 1, m, TP:T], LS), ALU.mult)
                            x.then_inc((ff_y, bank_free[1])[m], 1)
                        dve.wait_ge(ff_hi, i + 1)
                        TT(ffl[:, bass.ds(2 * i, 2), :], yb[:, :, :], ffh[:, bass.ds(2 * i, 2), :].bitcast(F32), ALU.subtract).then_inc(ff_lo, 1)

            def down(i):
                for k in range(44):
                    if i == 0 or k + LEAD < 44:
                        lo(down_base(i), k + LEAD)
                    if k % 11 == 10:
                        b = 4 * i + k // 11
                        kt = slice(2 * b, 2 * b + 2)
                        g2 = mod[:, 5 * KT + 2 * b:5 * KT + 2 * b + 2, :]
                        if b == 0:
                            dve.wait_ge(back_1, 16)
                        dve.wait_ge(used, down_base(i)[0] + k + 1 + FREE)
                        TT(dno[:, kt, 0:TP], ps[:, b % 2, :, 0:TP], g2[:, :, 0:1].to_broadcast([P, 2, TP]), ALU.mult).then_inc(x2_m, 1)
                        TT(seq3(dno[:, kt, TP:T], LS), seq3(ps[:, b % 2, :, TP:T], LS), rep3(g2[:, :, 1:NB], LS), ALU.mult).then_inc(bank_free[b % 2], 1)
                        dve.wait_ge(bank_free[b % 2], N_DOWN[1] + b // 2 + 1 + FREE)
                        TT(x1f[:, kt, :], x1f[:, kt, :], dno[:, kt, :], ALU.add).then_inc(x2_a, 1)
            down(0)
            down(1)
            dve.wait_ge(rs_done, 6)
            for kt in range(KT):
                STT(yT[:, kt, :], x1f[:, kt, :], par[:, 1, 32 + kt:33 + kt], rstd[:, :], ALU.mult, ALU.mult).then_inc(y_w, 1)
            for e in range(1, 12, 2):
                dve.wait_ge(y_t, e + 1)
                dve.wait_ge(y_c, e)
                w = P if e < 8 else TS
                nc.vector.tensor_copy(ytm[0:w, e // 4, 512 * (e % 4):512 * (e % 4) + 512], R[0:w, 1 + e % 3, :]).then_inc(y_c, 1)

        @block.gpsimd
        def _(pool):
            G, SEL = nc.gpsimd.tensor_tensor, nc.gpsimd.affine_select
            for s in (hg["out"], ml["out"], x1_acc, ab_tail):
                pool.sem_inc(s, FREE)
            cnt = [0]

            def cst_(ins):
                cnt[0] += 1
                ins.then_inc(const, 1)
                pool.wait_ge(const, cnt[0])
            cst_(nc.gpsimd.memset(ident[:, :], 0.0))
            cst_(SEL(out=ident[:, :], in_=ident[:, :], compare_op=ALU.not_equal, fill=1.0, base=0, pattern=[[-1, P]], channel_multiplier=1))
            cst_(nc.gpsimd.memset(ones[:, :], 1.0))
            cst_(nc.gpsimd.memset(ones8[:, :], 1.0))
            cst_(nc.gpsimd.memset(epsc[:, :], EPS))
            cst_(nc.gpsimd.memset(onec[:, :], 1.0))
            cst_(nc.gpsimd.memset(sel[:, :], 0.0))
            for part in range(2):
                cst_(SEL(out=sel[:, :], in_=sel[:, :], compare_op=ALU.not_equal, fill=1.0, base=-NB * part, pattern=[[-1, NB]], channel_multiplier=1))
            cst_(nc.gpsimd.memset(reset[:, :], 1.0))
            cst_(nc.gpsimd.memset(seq(reset[:, 0:TP], SUB)[:, :, 0:1], 0.0))
            cst_(nc.gpsimd.memset(seq(reset[:, TP:T], LS)[:, :, 0:1], 0.0))
            cst_(nc.gpsimd.memset(reset8[:, 0, :], 1.0))
            cst_(nc.gpsimd.memset(seq(reset8[:, 0, TP:T], LS)[:, :, 0:1], 0.0))
            cst_(nc.gpsimd.memset(reset8[:, 1, :], 0.0))
            cst_(nc.gpsimd.memset(reset8[:, 1, 0:1], NEG))
            cst_(nc.gpsimd.memset(seq(reset8[:, 1, TP:T], LS)[:, :, 0:1], NEG))
            for m, im, n, sub in ((maskf, hmask, P, SUB), (maskf_s, hmask_s, TS, LS)):
                cst_(nc.gpsimd.memset(m[:, :], 1.0))
                cst_(SEL(out=m[:, :], in_=m[:, :], compare_op=ALU.is_ge, fill=0.0, base=0, pattern=[[1, n]], channel_multiplier=-1))
                cst_(SEL(out=seq(m[:, :], sub), in_=seq(m[:, :], sub), compare_op=ALU.is_ge, fill=0.0, base=0, pattern=[[-sub, n // sub], [0, sub]], channel_multiplier=1))
                cst_(nc.gpsimd.tensor_copy(im[:, :], m[:, :]))
            cst_(nc.gpsimd.memset(amask[:, :], 0.0))
            cst_(SEL(out=amask[:, :], in_=amask[:, :], compare_op=ALU.is_ge, fill=NEG, base=0, pattern=[[1, TP]], channel_multiplier=-1))
            cst_(nc.gpsimd.tensor_scalar(amask_s[:, :], maskf_s[:, :], -NEG, NEG, ALU.mult, ALU.add))
            cst_(nc.gpsimd.memset(bmask[:, :], 1.0))
            cst_(SEL(out=bmask[:, :], in_=bmask[:, :], compare_op=ALU.is_ge, fill=0.0, base=0, pattern=[[-LS, NS]], channel_multiplier=1))
            cst_(SEL(out=bmask[:, :], in_=bmask[:, :], compare_op=ALU.is_ge, fill=0.0, base=LS - 1, pattern=[[LS, NS]], channel_multiplier=-1))
            assert cnt[0] == CONST_ALL
            cst_(nc.gpsimd.memset(lnms[:, :], 0.0))
            for kt in range(KT):
                if kt % 4 == 0:
                    pool.wait_ge(sq_done, kt // 4 + 1)
                if kt:
                    pool.wait_ge(x_sum, kt)
                G(lnms[:, :], lnms[:, :], merged[:, kt, :], ALU.add).then_inc(x_sum, 1)
            pool.wait_ge(x_c, KT + X_FREE)
            for half in range(2):
                pool.dma_start(xT_spill[:, half * KT * T // 2:(half + 1) * KT * T // 2],
                               xT[:, 8 * half:8 * half + 8, :].rearrange("p a b -> p (a b)")).then_inc(ml["st"], 16)
            pool.wait_ge(row_d, ROW_WK)
            with nc.allow_non_contiguous_dma(reason="72 values"):
                pool.dma_start(m_p[0].rearrange("b h -> h b"), merged[0:MH, 11, 0:1]).then_inc(hg["st"], 16)
                pool.dma_start(m_s[0].rearrange("b h -> h b"), merged[0:MH, 11, 1:NB]).then_inc(hg["st"], 16)
            pool.wait_ge(xlo, 4)
            pool.wait_ge(ml["st"], 32)
            pool.wait_ge(hg["st"], 32)
            pool.wait_ge(cv_c, 2)
            pool.wait_ge(gmm, 1)
            pool.wait_ge(row_t, 1)
            nc.gpsimd.memset(PT[:, :, :], 0.0).then_inc(hg["zero"], 1)
            nc.gpsimd.memset(PTs[:, :], 0.0).then_inc(hg["zero"], 1)
            nc.gpsimd.memset(Vx[:, :, :, :], 0.0).then_inc(hg["zero"], 1)
            pool.wait_ge(hg["zero"], 3)

            def hg_prologue(i):
                pool.wait_ge(hg["sig"], 4 * (i + 1))
                pool.wait_ge(hg["out"], 4 * i + FREE)
                G(W[:, 3], W[:, 3], W[:, 4], ALU.mult).then_inc(hg["pre"], 1)
                nc.gpsimd.tensor_copy(W[:, 2], S[:, 2]).then_inc(hg["pre"], 1)

            def hg_step(j, o, n, i):
                h = n
                if o == 2:
                    count = known(pool, 32 * (n + 1))
                    pool.wait_ge(const, CONST_ALL)
                    pool.wait_ge(hg["st"], count)
                    pool.dma_start(S0[:, :, :], state_hgrn[0].rearrange("b h k v -> h k b v")[bass.ds(h, 1)].rearrange("o k b v -> (o k) b v")).then_inc(hg["s0"], 16)
                if o == 1:
                    pool.wait_ge(hg["qk"], 2 * (n + 1))
                    G(seq(kh[:, 0:TP], SUB), seq(kt_[:, 0:TP], SUB), seq(e1[:, 0:TP], SUB)[:, :, SUB - 1:SUB].to_broadcast([P, NSUB, SUB]), ALU.mult).then_inc(hg["dk"], 1)
                    G(seq(kh[:, TP:T], LS), seq(kt_[:, TP:T], LS), seq(e1[:, TP:T], LS)[:, :, LS - 1:LS].to_broadcast([P, NS, LS]), ALU.mult).then_inc(hg["dk"], 1)
                    G(seq(qs[:, :], SUB), seq(qt[:, 0:TP], SUB), rep_last(er[:, :], SUB), ALU.mult).then_inc(hg["dk"], 1)
                    G(dec[:, :], er[:, :], seq(e1[:, 0:TP], SUB)[:, :, SUB - 1], ALU.mult).then_inc(hg["dk"], 1)
                if o == 3:
                    count = known(pool, 4 * (n + 1))
                    pool.wait_ge(const, CONST_ALL)
                    pool.wait_ge(hg["tok"], count)
                    for u in range(4):
                        rows_ = slice(SUB * u, SUB * (u + 1))
                        nc.gpsimd.tensor_copy(Vx[rows_, :, u, :], Vt[rows_, :, :]).then_inc(hg["vx"], 1)
                    G(Vxs[:, :, :], mid(Vts[:, :], NS), rep_last(bmask[:, :], P), ALU.mult).then_inc(hg["vx"], 1)
                if o == 6:
                    pool.wait_ge(hg["o"], n + 1)
                    G(S0[:, :, :], S0[:, :, :], seq(e1[:, TP:T], LS)[:, :, LS - 1:LS].to_broadcast([P, NS, P]), ALU.mult).then_inc(hg["scaled"], 1)
                if o == 9:
                    pool.wait_ge(hg["y"], n + 1 + FREE)
                    G(merged[:, bass.ds(h, 1), :].rearrange("p a b -> p (a b)"), e1[:, :], W[:, 3, j, :], ALU.mult).then_inc(hg["out"], 1)
                    count = known(pool, n + 1 + FREE)
                    pool.wait_ge(const, CONST_ALL)
                    pool.wait_ge(hg["snew"], count)
                    pool.dma_start(hg_s[0].rearrange("b h k v -> h k b v")[bass.ds(h, 1)].rearrange("o k b v -> (o k) b v"), S0[:, :, :]).then_inc(hg["st"], 16)
                    pool.dma_start(hg_p[0, 0, bass.ds(h, 1)].rearrange("o k v -> (o k) v"), Sst[:, NSUB - 1, :]).then_inc(hg["st"], 16)

            def ml_prologue(i):
                count = known(pool, 4 * (i + 1))
                pool.wait_ge(const, CONST_ALL)
                pool.wait_ge(ml["sig"], count)
                pool.wait_ge(ml["out"], 4 * i + FREE)
                G(mW[:, 8:12, :], mW[:, 8:12, :], mS[:, 12:16, :], ALU.mult).then_inc(ml["pre"], 1)
                nc.gpsimd.tensor_copy(mW[:, 4:8, :], mS[:, 4:8, :]).then_inc(ml["pre"], 1)

            def ml_step(j, o, n, i):
                h = n
                if o == 2:
                    count = known(pool, 32 * (n + 1))
                    pool.wait_ge(const, CONST_ALL)
                    pool.wait_ge(ml["st"], count)
                    pool.dma_start(C0[:, :, :], state_mlstm_C[0].rearrange("b h k v -> h k b v")[bass.ds(h, 1)].rearrange("o k b v -> (o k) b v")).then_inc(ml["c0"], 16)
                if o == 5:
                    pool.wait_ge(ml["v"], 2 * (n + 1))
                    G(mVx[:, :, :], mid(mV[0:TS, 2, :], NS), rep_last(bmask[:, :], MV), ALU.mult).then_inc(ml["vx"], 1)
                if o == 7:
                    pool.wait_ge(ml["num"], n + 1)
                    G(C0[:, :, :], C0[:, :, :], rep_last(es[:, TS:TS + NS], MV), ALU.mult).then_inc(ml["cs"], 1)
                    G(ndec[:, :].rearrange("p (b a) -> p b a", a=1), es[:, TS:TS + NS].rearrange("p (b a) -> p b a", a=1), n0v[:, :, bass.ds(h, 1)], ALU.mult).then_inc(ml["cs"], 1)
                if o == 10:
                    pool.wait_ge(ml["y"], 2 * (n + 1))
                    G(hh[:, :, :], hh[:, :, :], mW[:, 8 + 2 * j:10 + 2 * j, :], ALU.mult).then_inc(ml["out"], 1)
                    pool.wait_ge(ml["out"], 2 * n + 1 + FREE)
                    mg = merged[:, bass.ds(2 * h, 2), :]
                    G(mg, mg, hh[:, :, :], ALU.add).then_inc(ml["out"], 1)
                if o == 11:
                    count = known(pool, n + 1 + FREE)
                    pool.wait_ge(const, CONST_ALL)
                    pool.wait_ge(ml["c2"], count)
                    pool.dma_start(C_s[0].rearrange("b h k v -> h k b v")[bass.ds(h, 1)].rearrange("o k b v -> (o k) b v"), C0[:, :, :]).then_inc(ml["st"], 16)
                    pool.dma_start(C_p[0, 0, bass.ds(h, 1)].rearrange("o k v -> (o k) v"), Cp[:, :]).then_inc(ml["st"], 16)

            n0v = par[:, 3, 44:108].rearrange("p (b h) -> p b h", h=MH)
            with pool.Fori(0, 3) as i:
                hg_prologue(i)
                for k in range(HG_STEP):
                    for j, o in HG_AT[k]:
                        hg_step(j, o, 4 * i + j, i)
            hg_prologue(3)
            for k in range(ML_STEP):
                for j, o in HG_AT_ML[k]:
                    hg_step(j, o, 12 + j, 3)
            pool.wait_ge(hg["st"], 32 * (HH + 1))
            with pool.Fori(0, 3) as i:
                ml_prologue(i)
                for k in range(ML_STEP):
                    for j, o in ML_AT[k]:
                        ml_step(j, o, 2 * i + j, i)
            ml_prologue(3)
            for k in range(ML_STEP):
                for j, o in ML_AT[k]:
                    ml_step(j, o, 6 + j, 3)
            pool.wait_ge(n_c, 1)
            pool.dma_start(n_p[0, 0], ntok[0:MH, :]).then_inc(st_n, 16)
            pool.dma_start(n_s[0].rearrange("b h d -> (b h) d"), ntok[MH:, :]).then_inc(st_n, 16)
            pool.wait_ge(ml["st"], 32 * (MH + 1))
            pool.dma_start(xT2[:].rearrange("p a b -> p (a b)"), xT_spill).then_inc(back_x, 16)
            nc.gpsimd.memset(sqacc[:, :, :], 0.0).then_inc(zab, 1)
            pool.wait_ge(zab, 1)
            with pool.Fori(0, 3) as i:
                pool.wait_ge(x1_sq, i + 1)
                pool.wait_ge(x1_acc, i + FREE)
                G(sqacc[:, :, :], sqacc[:, :, :], mixo[:, bass.ds(4 * i, 4), :], ALU.add).then_inc(x1_acc, 1)
            pool.wait_ge(x1_a, 8)
            pool.dma_start(x1_spill, xT2[:].rearrange("p a b -> p (a b)")).then_inc(spill_1, 16)
            pool.wait_ge(xlo, 12)
            pool.wait_ge(st_n, 32)
            nc.gpsimd.memset(abuf[:, :, 0:2], 0.0).then_inc(zab, 1)
            with pool.Fori(0, 22) as i:
                count = known(pool, 6 * i + FREE)
                pool.wait_ge(const, CONST_ALL)
                pool.wait_ge(ff_conv, count)
                leads = seq3(abuf[:, :, 2 + TP:AB], 2 + LS)
                pool.wait_ge(ab_tail, 2 * i + FREE)
                for m in range(2):
                    x = nc.gpsimd.tensor_copy(seq(abuf[:, m, 2 + TP:AB], 2 + LS)[:, :, 0:2], cst[:, bass.ds(2 * i + m, 1), :].rearrange("p o (b j) -> p (o b) j", j=2))
                x.then_inc(ab_lead, 1)
                count = known(pool, N_UP[1] + i + 1 + FREE)
                pool.wait_ge(const, CONST_ALL)
                pool.wait_ge(bank_free[0], count)
                nc.gpsimd.tensor_copy(tails[:, bass.ds(2 * i, 2), 0:2], abuf[:, :, TP:TP + 2]).then_inc(ab_tail, 1)
                for m in range(2):
                    x = nc.gpsimd.tensor_copy(tails[:, bass.ds(2 * i + m, 1), 2:].rearrange("p o (b j) -> p (o b) j", j=2), seq(abuf[:, m, 2 + TP:AB], 2 + LS)[:, :, LS:LS + 2])
                x.then_inc(ab_tail, 1)
            pool.wait_ge(used, N_DOWN[0] + FREE)
            pool.dma_start(x1f[:].rearrange("p a b -> p (a b)"), x1_spill).then_inc(back_1, 16)
            pool.wait_ge(ff_lo, 22 + FREE)
            nc.gpsimd.memset(sqf[:, :, :], 0.0).then_inc(zab, 1)
            pool.wait_ge(zab, 3)
            for b in range(8):
                for g in range(11):
                    if b < 2 and g // 6 == b:
                        pool.wait_ge(tl_c, g + 1)
                        pool.dma_start(cv_p[0, 0, :, 512 * g:512 * g + 512], cts[0:2, g % 2, :]).then_inc(st_cv[g % 2], 16)
                        pool.dma_start(cv_s[0].rearrange("b j f -> (b j) f")[:, 512 * g:512 * g + 512], cts[2:2 + NS * 2, g % 2, :]).then_inc(st_cv[g % 2], 16)
                pool.wait_ge(x2_sq, b + 1)
                pool.wait_ge(x2_acc, b)
                G(sqf[:, :, :], sqf[:, :, :], sqd[:, :, :], ALU.add).then_inc(x2_acc, 1)


_INS = ['x_prompt', 'x_sample', 'c_prompt', 'c_sample', 'state_hgrn', 'state_mlstm_C', 'state_mlstm_n', 'state_mlstm_m',
        'state_conv', 'ada_w', 'ada_b', 'w_in', 'hg_lb_logits', 'hg_norm_w', 'ml_i_bias', 'ml_f_bias', 'ml_norm_w', 'w_out',
        'conv_w', 'conv_b', 'w_up', 'w_down', 'final_norm_w']
_OUTS = [(1, 256, 2048), (8, 4, 2048), (1, 1, 16, 128, 128), (1, 8, 16, 128, 128), (1, 1, 8, 128, 256), (1, 8, 8, 128, 256),
         (1, 1, 8, 128), (1, 8, 8, 128), (1, 1, 8), (1, 8, 8), (1, 1, 2, 5632), (1, 8, 2, 5632)]


def kernel(**inputs):
    import concourse.bacc as _bacc
    from concourse.bass_utils import run_bass_kernel_spmd as _run

    nc = _bacc.Bacc("TRN2", target_bir_lowering=False, num_devices=1)
    arrays, args = {}, []
    for name in _INS:
        a = np.ascontiguousarray(inputs[name])
        arrays[f"in_{name}"] = a
        args.append(nc.dram_tensor(f"in_{name}", a.shape, mybir.dt.from_np(a.dtype), kind="ExternalInput").ap())
    for i, shape in enumerate(_OUTS):
        args.append(nc.dram_tensor(f"out_{i}", shape, F32, kind="ExternalOutput").ap())
    build(nc, *args)
    r = _run(nc, [arrays], core_ids=[0])
    return tuple(r.results[0][f"out_{i}"] for i in range(len(_OUTS)))
```
